# Optimizing a Trainium2 kernel written in Bass

```python
import jax, jax.numpy as jnp
from jax import lax
import numpy as np

D_MODEL = 1024
BATCH = 1
SEQ = 512
DEPTH = 1

CHUNK = 64
MEM_LEN = 256
MIX_DIM = D_MODEL
GLA_HEADS = 4
GLA_DV = MIX_DIM // 2 // GLA_HEADS
GLA_DK = GLA_DV // 2
GLA_GATE_RANK = 16
GLA_TAU = 16.0
SB_HEADS = 8
SB_HD = MIX_DIM // 2 // SB_HEADS
SB_BLOCK = 128
MEM_HEADS = 4
MEM_HD = D_MODEL // MEM_HEADS
N_EXPERTS = 32
TOP_K = 4
D_EXPERT = D_MODEL
SWIGLU_LIMIT = 7.0
SWIGLU_ALPHA = 1.702
EXPERT_BLOCK = 128
EPS = 1e-5

Q_G = GLA_HEADS * GLA_DK
V_G = GLA_HEADS * GLA_DV
SB_W = SB_HEADS * SB_HD
IN_SPLITS = (Q_G, Q_G, V_G, GLA_GATE_RANK, V_G, SB_W, SB_W, SB_W)
IN_DIM = sum(IN_SPLITS)
IN_OFFSETS = tuple(int(v) for v in np.cumsum(IN_SPLITS)[:-1])

kernel_name = "hybrid_gla_stickbreak_moe_block"

def rmsnorm(x, g):
    xf = x.astype(jnp.float32)
    y = xf * lax.rsqrt(jnp.mean(xf * xf, axis=-1, keepdims=True) + EPS)
    return (y * g.astype(jnp.float32)).astype(x.dtype)

def gla_group(q, k, v, log_a):
    B, S, H, dk = q.shape
    dv = v.shape[-1]
    nc = S // CHUNK
    qc = q.reshape(B, nc, CHUNK, H, dk)
    kc = k.astype(jnp.float32).reshape(B, nc, CHUNK, H, dk)
    vc = v.astype(jnp.float32).reshape(B, nc, CHUNK, H, dv)
    G = jnp.cumsum(log_a.astype(jnp.float32).reshape(B, nc, CHUNK, H, dk), axis=2)
    G_end = G[:, :, -1]
    k_dec = kc * jnp.exp(G_end[:, :, None] - G)
    U = jnp.einsum('bnshd,bnshv->bnhdv', k_dec, vc)
    decay = jnp.exp(G_end)

    def step(state, inp):
        d, u = inp
        state = d[..., None] * state + u
        return state, state

    init = jnp.zeros((B, H, dk, dv), jnp.float32)
    _, states = lax.scan(step, init, (jnp.moveaxis(decay, 1, 0), jnp.moveaxis(U, 1, 0)))
    states = jnp.moveaxis(states, 0, 1)
    o = jnp.einsum('bnthd,bnhdv->bnthv', qc.astype(jnp.float32), states)
    return o.reshape(B, S, H, dv).astype(q.dtype)

def stick_breaking_group(q, k, v):
    B, S, H, d = q.shape
    scale = d ** -0.5
    outs = []
    for i in range(S // SB_BLOCK):
        t0 = i * SB_BLOCK
        L = t0 + SB_BLOCK
        qb = q[:, t0:L]
        kb = k[:, :L]
        vb = v[:, :L].astype(jnp.float32)
        z = jnp.einsum('bthd,bshd->bhts', qb, kb).astype(jnp.float32) * scale
        t_pos = t0 + jnp.arange(SB_BLOCK)
        s_pos = jnp.arange(L)
        mask = s_pos[None, :] < t_pos[:, None]
        log_1mb = jnp.where(mask, jax.nn.log_sigmoid(-z), 0.0)
        suffix = lax.cumsum(log_1mb, axis=3, reverse=True) - log_1mb
        A = jnp.where(mask, jnp.exp(jax.nn.log_sigmoid(z) + suffix), 0.0)
        outs.append(jnp.einsum('bhts,bshd->bthd', A, vb))
    return jnp.concatenate(outs, axis=1).astype(q.dtype)

def memory_cross_attention(hq, m, w_mq, w_mk, w_mv, w_mo):
    B, S, _ = hq.shape
    M = m.shape[1]
    q = (hq @ w_mq).reshape(B, S, MEM_HEADS, MEM_HD)
    k = (m @ w_mk).reshape(B, M, MEM_HEADS, MEM_HD)
    v = (m @ w_mv).reshape(B, M, MEM_HEADS, MEM_HD)
    s = jnp.einsum('bthd,bmhd->bhtm', q, k).astype(jnp.float32) * (MEM_HD ** -0.5)
    p = jax.nn.softmax(s, axis=-1).astype(v.dtype)
    o = jnp.einsum('bhtm,bmhd->bthd', p, v).reshape(B, S, MEM_HEADS * MEM_HD)
    return o @ w_mo

def moe_ffn(h, w_router, b_router, w_gu, b_gu, w_down, b_down):
    B, S, D = h.shape
    N = B * S
    hf = h.reshape(N, D)
    logits = (hf @ w_router + b_router).astype(jnp.float32)
    top_vals, top_idx = lax.top_k(logits, TOP_K)
    gates = jax.nn.softmax(top_vals, axis=-1).astype(h.dtype)

    NK = N * TOP_K
    flat_e = top_idx.reshape(NK).astype(jnp.int32)
    flat_w = gates.reshape(NK)
    flat_tok = jnp.repeat(jnp.arange(N, dtype=jnp.int32), TOP_K)
    order = jnp.argsort(flat_e)
    sorted_e = flat_e[order]
    counts = jnp.bincount(flat_e, length=N_EXPERTS).astype(jnp.int32)
    padded = ((counts + EXPERT_BLOCK - 1) // EXPERT_BLOCK) * EXPERT_BLOCK
    pad_end = jnp.cumsum(padded)
    pad_start = pad_end - padded
    start = jnp.cumsum(counts) - counts
    rank = jnp.arange(NK, dtype=jnp.int32) - start[sorted_e]
    dest = pad_start[sorted_e] + rank

    n_blocks = -(-(NK + N_EXPERTS * (EXPERT_BLOCK - 1)) // EXPERT_BLOCK)
    M = n_blocks * EXPERT_BLOCK
    slot_tok = jnp.full((M,), N, jnp.int32).at[dest].set(flat_tok[order])
    slot_w = jnp.zeros((M,), h.dtype).at[dest].set(flat_w[order])
    block_start = jnp.arange(n_blocks, dtype=jnp.int32) * EXPERT_BLOCK
    block_expert = jnp.minimum(jnp.sum(block_start[:, None] >= pad_end[None, :], axis=1), N_EXPERTS - 1).astype(jnp.int32)

    h_pad = jnp.concatenate([hf, jnp.zeros((1, D), hf.dtype)], axis=0)
    xs = h_pad[slot_tok].reshape(n_blocks, EXPERT_BLOCK, D)

    def expert_block(args):
        xb, e = args
        gu = xb @ w_gu[e] + b_gu[e]
        gate, lin = gu[:, :D_EXPERT], gu[:, D_EXPERT:]
        gate = jnp.minimum(gate, SWIGLU_LIMIT)
        lin = jnp.clip(lin, -SWIGLU_LIMIT, SWIGLU_LIMIT)
        act = (lin + 1.0) * (gate * jax.nn.sigmoid(SWIGLU_ALPHA * gate))
        return act @ w_down[e] + b_down[e]

    ys = lax.map(expert_block, (xs, block_expert)).reshape(M, D) * slot_w[:, None]
    out = jax.ops.segment_sum(ys, slot_tok, num_segments=N + 1)[:N]
    return out.reshape(B, S, D)

def setup_inputs(seed: int = 0) -> dict:
    key = jax.random.key(seed)
    ks = jax.random.split(key, 24)

    def nrm(k, shape, scale):
        return jax.random.normal(k, shape, jnp.float32) * scale

    def gain(k, shape):
        return 1.0 + 0.05 * jax.random.normal(k, shape, jnp.float32)

    L = DEPTH
    return {
        'x': nrm(ks[0], (BATCH, SEQ, D_MODEL), 1.0),
        'mem': nrm(ks[1], (BATCH, MEM_LEN, D_MODEL), 1.0),
        'g_mix': gain(ks[2], (L, D_MODEL)),
        'w_in': nrm(ks[3], (L, D_MODEL, IN_DIM), D_MODEL ** -0.5),
        'w_gla_gate': nrm(ks[4], (L, GLA_GATE_RANK, Q_G), GLA_GATE_RANK ** -0.5),
        'b_gla_gate': nrm(ks[5], (L, Q_G), 0.5),
        'g_gla_head': gain(ks[6], (L, GLA_DV)),
        'w_out': nrm(ks[7], (L, MIX_DIM, D_MODEL), MIX_DIM ** -0.5),
        'g_mem_q': gain(ks[8], (L, D_MODEL)),
        'g_mem_kv': gain(ks[9], (L, D_MODEL)),
        'w_mq': nrm(ks[10], (L, D_MODEL, MEM_HEADS * MEM_HD), D_MODEL ** -0.5),
        'w_mk': nrm(ks[11], (L, D_MODEL, MEM_HEADS * MEM_HD), D_MODEL ** -0.5),
        'w_mv': nrm(ks[12], (L, D_MODEL, MEM_HEADS * MEM_HD), D_MODEL ** -0.5),
        'w_mo': nrm(ks[13], (L, MEM_HEADS * MEM_HD, D_MODEL), (MEM_HEADS * MEM_HD) ** -0.5),
        'g_ffn': gain(ks[14], (L, D_MODEL)),
        'w_router': nrm(ks[15], (L, D_MODEL, N_EXPERTS), D_MODEL ** -0.5),
        'b_router': nrm(ks[16], (L, N_EXPERTS), 0.01),
        'w_gu': nrm(ks[17], (L, N_EXPERTS, D_MODEL, 2 * D_EXPERT), D_MODEL ** -0.5),
        'b_gu': nrm(ks[18], (L, N_EXPERTS, 2 * D_EXPERT), 0.02),
        'w_down': nrm(ks[19], (L, N_EXPERTS, D_EXPERT, D_MODEL), D_EXPERT ** -0.5),
        'b_down': nrm(ks[20], (L, N_EXPERTS, D_MODEL), 0.02),
        'g_final': gain(ks[21], (D_MODEL,)),
    }

def reference(x, mem, g_mix, w_in, w_gla_gate, b_gla_gate, g_gla_head, w_out,
              g_mem_q, g_mem_kv, w_mq, w_mk, w_mv, w_mo,
              g_ffn, w_router, b_router, w_gu, b_gu, w_down, b_down, g_final):
    B, S, _ = x.shape
    for l in range(DEPTH):
        h = rmsnorm(x, g_mix[l])
        proj = h @ w_in[l]
        qg, kg, vg, glr, rg, qs, ks_, vs = jnp.split(proj, IN_OFFSETS, axis=-1)

        log_a = jax.nn.log_sigmoid((glr @ w_gla_gate[l] + b_gla_gate[l]).astype(jnp.float32)) / GLA_TAU
        o_gla = gla_group(qg.reshape(B, S, GLA_HEADS, GLA_DK) * (GLA_DK ** -0.5),
                          kg.reshape(B, S, GLA_HEADS, GLA_DK),
                          vg.reshape(B, S, GLA_HEADS, GLA_DV),
                          log_a.reshape(B, S, GLA_HEADS, GLA_DK))
        o_gla = rmsnorm(o_gla, g_gla_head[l]).reshape(B, S, V_G) * jax.nn.silu(rg)

        o_sb = stick_breaking_group(qs.reshape(B, S, SB_HEADS, SB_HD),
                                    ks_.reshape(B, S, SB_HEADS, SB_HD),
                                    vs.reshape(B, S, SB_HEADS, SB_HD)).reshape(B, S, SB_W)

        x = x + jnp.concatenate([o_gla, o_sb], axis=-1) @ w_out[l]

        x = x + memory_cross_attention(rmsnorm(x, g_mem_q[l]), rmsnorm(mem, g_mem_kv[l]),
                                       w_mq[l], w_mk[l], w_mv[l], w_mo[l])

        x = x + moe_ffn(rmsnorm(x, g_ffn[l]), w_router[l], b_router[l],
                        w_gu[l], b_gu[l], w_down[l], b_down[l])
    return rmsnorm(x, g_final)


_drawn_inputs = setup_inputs


def setup_inputs(seed=0):
    import zlib

    import numpy as np

    out = dict(_drawn_inputs(seed))
    spreads = {}
    factors = {'b_gu': 5.846, 'b_down': 6.682}
    for name, (base, spread) in spreads.items():
        noise = np.random.default_rng([zlib.crc32(name.encode()), seed]).standard_normal(out[name].shape)
        drawn = base * np.exp(spread * noise) if base else spread * noise
        out[name] = __import__('jax').numpy.asarray(drawn.astype(out[name].dtype))
    for name, factor in factors.items():
        out[name] = (out[name] * factor).astype(out[name].dtype)
    return out
```

```python
from contextlib import ExitStack

import numpy as np

import concourse.bass as bass
from concourse import mybir

F32 = mybir.dt.float32
F32R = mybir.dt.float32r
I32 = mybir.dt.int32
U32 = mybir.dt.uint32
ALU = mybir.AluOpType
ACT = mybir.ActivationFunctionType
AX = mybir.AxisListType

P = 128
T = 512
TT = T // P
D = 1024
KT = D // P
M = 256
MT_ = M // P
EPS = 1e-5
GLA_CHUNK = 64
N_CHUNKS = T // GLA_CHUNK
TAU = 16.0
SB_HEADS = 8
MEM_HEADS = 4
E = 32
K = 4
C = 96
OVER = T // C
MAX_ITEMS = E + T * K // C
COLS = MAX_ITEMS + 1
PADS = C
LIMIT = 7.0
ALPHA = 1.702
QG, KG, VG, GLR, RG, QS, KS, VS = 0, 256, 512, 1024, 1040, 1552, 2064, 2576


class Banks:

    def __init__(self):
        self.names, self.bank, self.taker, self.before = [], {}, {}, {}
        self.last, self.next = {}, 0

    def add(self, name, taker, pool=tuple(range(8))):
        b = pool[self.next % len(pool)]
        self.next += 1
        self.before[name] = self.last.get(b)
        self.last[b] = name
        self.names.append(name)
        self.bank[name], self.taker[name] = b, taker

    def filled(self, name):
        return self.names.index(name) + 1

    def emptied(self, name):
        n = self.names.index(name)
        return sum(self.taker[x] == self.taker[name] for x in self.names[:n + 1])


FILL = [
    [("qg", 0)], [("qg", 1), ("kg", 0)],
    [("kg", 1), ("kg", 2)], [("kg", 3), ("vg", 0)],
    [("glrT",), ("vg", 1)], [("gz", 0), ("gz", 1), ("vg", 2)],
    [("vg", 3)], [("gs", 0), ("gs", 1), ("gend",), ("rg", 0)],
    [("U", 0), ("U", 1), ("rg", 1)], [("U", 2), ("U", 3), ("rg", 2)],
    [("rg", 3)], [("O", 0, 0), ("O", 0, 1)],
    [("O", 1, 0), ("O", 1, 1)], [],
    [], [],
]
DVE_FILL = {"kg", "gz", "U", "rg", "O"}


def plan_banks():
    plan = Banks()
    plan.add(("gcols",), "dve")
    for k in range(KT):
        plan.add(("hT", k), "act" if k % 2 else "dve")
    for j in range(4):
        plan.add(("qs", j), "act" if j % 2 else "dve")
    for j in range(4):
        plan.add(("ks", j), "act" if j % 2 else "dve")
    plan.add(("bgu",), "act")
    for i in range(TT):
        plan.add(("vs", i), "act" if i % 2 else "dve", pool=(6, 7))
    for h in range(SB_HEADS):
        for part in (0, 1):
            for g in FILL[2 * h + part]:
                plan.add(g, "dve" if g[0] in DVE_FILL else "act", pool=(6, 7))
            if part == 1:
                plan.add(("av", h), "dve", pool=(6, 7))
    for f in range(4):
        plan.add(("gT", f), "act" if f % 2 else "dve")
    for i in range(TT):
        for half in range(2):
            plan.add(("y1", i, half), "dve")
    for kk in range(4):
        plan.add(("mT", kk), "dve")
    for c in range(4):
        plan.add(("km", c), "act" if c % 2 else "dve")
    for mi in range(MT_):
        for half in range(2):
            plan.add(("vm", mi, half), "act" if half else "dve")
    for k in range(KT):
        plan.add(("h2T", k), "act" if k % 2 else "dve")
    for j in range(8):
        plan.add(("qm", j), "act" if j % 2 else "dve")
    for i in range(TT):
        for hp in range(2):
            plan.add(("sc", i, hp), "act")
    for h in range(MEM_HEADS):
        for mt in range(MT_):
            plan.add(("pT", h, mt), "act" if mt else "dve")
    for h in range(MEM_HEADS):
        for dt in range(2):
            plan.add(("oc", h, dt), "act" if dt else "dve")
    for i in range(TT):
        for half in range(2):
            plan.add(("y2", i, half), "dve")
    for k in range(KT):
        plan.add(("h3T", k), "act" if k % 2 else "dve")
    plan.add(("logitsT",), "dve")
    plan.add(("logits",), "dve")
    plan.add(("ranks",), "dve")
    plan.add(("gatesT",), "dve")
    for i in range(TT):
        for half in range(2):
            plan.add(("bd", i, half), "dve")
    return plan


SB_SEG = [(0, 0, 0), (1, 0, 512), (2, 0, 896), (2, 256, 1152)]
SB_COLS = 1280


def build(nc, x, mem, g_mix, w_in, w_gla_gate, b_gla_gate, g_gla_head, w_out, g_mem_q, g_mem_kv,
          w_mq, w_mk, w_mv, w_mo, g_ffn, w_router, b_router, w_gu, b_gu, w_down, b_down, g_final, out):
    plan = plan_banks()
    rows_dram = nc.dram_tensor("rows_scratch", [T, D], F32).ap()
    acc_dram = nc.dram_tensor("acc_scratch", [T + PADS, D], F32).ap()
    table_dram = nc.dram_tensor("table_scratch", [C * COLS, 2], F32).ap()

    with ExitStack() as ctx:
        def sb(name, shape, dt=F32):
            return ctx.enter_context(nc.sbuf_tensor(name, shape, dt))

        def sem(name):
            return ctx.enter_context(nc.semaphore(name))

        ring = sb("ring", [P, 6, 4096])
        scratch = ring[:, 4:6, :].rearrange("p a b -> p (a b)")
        x_at = nc.sbuf_base
        X = sb("X", [P, TT, D])
        A = sb("A", [P, 4096])
        h_at = nc.sbuf_base
        H = sb("H", [P, KT, T])
        MIX = sb("MIX", [P, KT, T])
        v_at = nc.sbuf_base
        VSb = sb("VSb", [P, 2048])
        VGb = sb("VGb", [P, 2048])
        RGb = sb("RGb", [P, 2048])
        STb = sb("STb", [P, 2048])
        q_at = nc.sbuf_base
        QGb = sb("QGb", [P, 1024])
        KDb = sb("KDb", [P, 1024])
        ident = sb("ident", [P, P])
        neg_tri = sb("neg_tri", [P, P])
        neg_ones = sb("neg_ones", [P, P])
        chunk_after = sb("chunk_after", [P, P])
        before = sb("before", [P, P])
        ones = sb("ones", [P, P])
        chunk_of = sb("chunk_of", [P, 2])
        one_col = sb("one_col", [P, 1])
        eps_col = sb("eps_col", [P, 1])
        bguT = sb("bguT", [P, 16, E])
        gcols = sb("gcols", [P, 4 * KT + 1])
        w_glr = sb("w_glr", [P, KT, 16])
        w_gate = sb("w_gate", [17, 256])
        ssq = sb("ssq", [P, 32])
        rstd = sb("rstd", [P, 32])
        decay = sb("decay", [P, 16])

        xn = A[:, :].rearrange("p (i d) -> p i d", i=TT)
        gain_rows = RGb[0:33, 0:P]
        bgu_rows = MIX[0:E, 0:4, :].rearrange("p a b -> p (a b)")
        prefill = STb[0:C, 0:2 * COLS].rearrange("p (n two) -> p n two", two=2)
        qsT = A[:, 0:2048].rearrange("p (j t) -> p j t", j=4)
        ksT = A[:, 2048:4096].rearrange("p (j t) -> p j t", j=4)
        vs = VSb[:, :].rearrange("p (i c) -> p i c", i=TT)
        sb_w = [scratch[:, 2560 * b:2560 * b + SB_COLS] for b in range(2)]
        sb_sp = [scratch[:, 2560 * b + SB_COLS:2560 * b + 2 * SB_COLS] for b in range(2)]
        kg = scratch[:, 5120:5120 + 1088].rearrange("p (i c) -> p i c", i=TT)
        log_a = scratch[:, 6208:6208 + 1024].rearrange("p (i c) -> p i c", i=TT)
        silu_t = scratch[:, 7232:7232 + 512]
        glrT = KDb[0:32, 0:512]
        kd = KDb[:, :].rearrange("p (i c) -> p i c", i=TT)
        vg = VGb[:, :].rearrange("p (i c) -> p i c", i=TT)
        og = VGb[:, :].rearrange("p (i h d) -> p i h d", i=TT, h=4)
        rg = RGb[:, :].rearrange("p (i c) -> p i c", i=TT)
        qg = QGb[:, :].rearrange("p (j t) -> p j t", j=2)
        state = STb[:, :].rearrange("p (c j d) -> p c j d", c=N_CHUNKS, j=2)
        gla_junk = MIX[:, 0, 0:P]
        mem_rows = VSb[:, :].rearrange("p (i d) -> p i d", i=MT_)
        mem_junk = STb[:, 0:D]
        mT = VGb[:, :].rearrange("p (k m) -> p k m", k=KT)
        kmT = RGb[:, :].rearrange("p (k m) -> p k m", k=KT)
        vm = STb[:, :].rearrange("p (i d) -> p i d", i=MT_)
        qmT = A[:, :].rearrange("p (j t) -> p j t", j=8)
        probs = scratch[:, 0:4096].rearrange("p (i h m) -> p i h m", i=TT, h=MEM_HEADS)
        probsT = scratch[:, 4096:8192].rearrange("p (h m t) -> p h m t", h=MEM_HEADS, m=MT_)
        neg_max = QGb[:, 0:16]
        row_sum = QGb[:, 16:32]
        w_rt = QGb[:, 32:32 + KT * E].rearrange("p (k e) -> p k e", k=KT)
        b_rt = QGb[0:E, 288:289]
        logitsT = STb[0:E, 0:T]
        logits = QGb[:, 320:448].rearrange("p (i e) -> p i e", i=TT)
        top_v = QGb[:, 448:480].rearrange("p (i k) -> p i k", i=TT)
        top_i = QGb[:, 480:512].rearrange("p (i k) -> p i k", i=TT)
        top_f = QGb[:, 512:528].rearrange("p (i k) -> p i k", i=TT)
        gate4 = QGb[:, 528:544].rearrange("p (i k) -> p i k", i=TT)
        dest_f = QGb[:, 544:560]
        dest_i = QGb[:, 560:576]
        payload = QGb[:, 576:608].rearrange("p (n two) -> p n two", two=2)
        gsum = QGb[:, 608:612]
        tokid = QGb[:, 612:616]
        iota_e = QGb[:, 616:648]
        iota_o = QGb[:, 648:648 + 32]
        picks = QGb[:, 680:808].rearrange("p (i e) -> p i e", i=TT)
        ranks = QGb[:, 808:968]
        neg_v0 = QGb[:, 968:972]
        over_e = VSb[:, 0:32]
        over_before = VSb[:, 32:64]
        over_upto = VSb[:, 64:96]
        block_f = VSb[:, 96:224].rearrange("p (i e) -> p i e", i=TT)
        slot_f = VSb[:, 224:352].rearrange("p (i e) -> p i e", i=TT)
        item_f = VSb[:, 352:480].rearrange("p (i e) -> p i e", i=TT)
        has_f = VSb[:, 480:608].rearrange("p (i e) -> p i e", i=TT)
        item_e = VSb[:, 608:608 + 64]
        n_items_f = VSb[:, 672:673]
        gate_e = VSb[:, 704:832].rearrange("p (i e) -> p i e", i=TT)
        gate_eT = VSb[:, 832:960]
        bdown = VSb[:, 1024:2048]
        onehot = VGb[:, 0:512].rearrange("p (n e) -> p n e", n=16)
        oh_gate = VGb[:, 512:1024].rearrange("p (n e) -> p n e", n=16)
        oh_dest = VGb[:, 1024:1536].rearrange("p (n e) -> p n e", n=16)
        earlier_e = RGb[:, 0:1024].rearrange("p (a b) -> p a b", a=E)
        over_m = RGb[:, 1024:2048].rearrange("p (a b) -> p a b", a=E)
        table = KDb[0:C, 0:2 * COLS].rearrange("p (n two) -> p n two", two=2)
        acc_row = KDb[0:C, 108:108 + COLS].bitcast(I32)
        src_row = KDb[0:C, 164:164 + COLS].bitcast(I32)
        item_expert = KDb[:, 220:220 + 64].bitcast(I32)
        n_items_i = KDb[:, 284:285].bitcast(I32)
        gather_idx = KDb[0:C, 286:287].bitcast(I32)
        scatter_idx = KDb[0:C, 287:288].bitcast(I32)
        gate_cur = KDb[0:C, 288:289]
        bias_cur = KDb[:, 296:312]
        src_f = KDb[0:C, 320:320 + COLS]
        x_rows = H[0:C, 0:2, :].rearrange("p a b -> p (a b)")
        y_rows = H[0:C, 2:4, :].rearrange("p a b -> p (a b)")
        g_fin = H[:, 4:6, :].rearrange("p a b -> p (a b)")
        fl = MIX[:, :, :].rearrange("p a b -> p (a b)")
        xsT = fl[:, 0:768].rearrange("p (k c) -> p k c", k=KT)
        act_f = fl[:, 768:1152].rearrange("p (k c) -> p k c", k=4)
        gate_h = fl[:, 1536:1920].rearrange("p (k c) -> p k c", k=4)
        lin_h = fl[:, 1920:2304].rearrange("p (k c) -> p k c", k=4)
        sig_h = fl[:, 2304:2688].rearrange("p (k c) -> p k c", k=4)

        wd_hi = nc.alloc_sbuf_tensor_at("wd_hi", [P, KT, D], F32R, offset=x_at)
        wd_lo = nc.alloc_sbuf_tensor_at("wd_lo", [P, KT, D], F32R, offset=v_at)
        act_hi = nc.alloc_sbuf_tensor_at("act_hi", [P, KT, C], F32R, offset=h_at + 3 * D * 4)
        act_lo = nc.alloc_sbuf_tensor_at("act_lo", [P, KT, C], F32R, offset=q_at)

        psum = ctx.enter_context(nc.psum_tensor("psum", [P, 8, 512], F32))

        def bank(name):
            return psum[:, plan.bank[name], :]

        s_const = sem("constants_built")
        s_x = [sem(f"x_tile_loaded_{i}") for i in range(TT)]
        s_gain = sem("gain_rows_loaded")
        s_bgu = sem("b_gu_rows_loaded")
        s_small = sem("gla_small_loaded")
        s_mem = sem("mem_rows_loaded")
        s_route_w = sem("router_weights_loaded")
        s_bd = sem("b_down_loaded")
        s_gfin = sem("g_final_loaded")
        s_w = [sem(f"ring_slot_loaded_{s}") for s in range(6)]
        s_full = sem("psum_bank_filled")
        s_act_took = sem("bank_emptied_by_act")
        s_dve_took = sem("bank_emptied_by_dve")
        s_act = sem("act_step")
        s_dve = sem("dve_step")
        s_pool = sem("pool_step")
        s_xn = sem("normed_rows_ready")
        s_res = sem("residual_tile_updated")
        s_sbz = sem("sb_scores_ready")
        s_sbln = sem("sb_log_ready")
        s_sbsp = sem("sb_softplus_ready")
        s_sbspm = sem("sb_softplus_masked")
        s_sbsuf = sem("sb_suffix_ready")
        s_sba = sem("sb_weights_ready")
        s_sbam = sem("sb_weights_masked")
        s_gzln = sem("gate_log_ready")
        s_loga = sem("log_decay_ready")
        s_kexp = sem("key_decay_ready")
        s_kd = sem("decayed_keys_ready")
        s_rgexp = sem("silu_exp_ready")
        s_osq = sem("gla_bank_squared")
        s_ogr = sem("gla_rstd_ready")
        s_og = sem("gla_rows_ready")
        s_memn = sem("mem_rows_normed")
        s_smax = sem("score_max_ready")
        s_prob = sem("probs_normalized")
        s_rowsout = sem("rows_stored")
        s_accinit = sem("accumulator_stored")
        s_x2b = sem("residual_with_bias_ready")
        s_negv = sem("top_value_negated")
        s_gexp = sem("gate_exp_ready")
        s_picks = sem("picks_ready")
        s_pay = sem("payload_ready")
        s_pref = sem("table_prefilled")
        s_tab = sem("table_scattered")
        s_tabl = sem("table_loaded")
        s_items = sem("items_ready")
        s_gidx = sem("gather_index_ready")
        s_xrow = sem("item_rows_gathered")
        s_xt = sem("item_rows_transposed")
        s_xs = sem("item_xT_ready")
        s_gu = sem("item_gu_bank_filled")
        s_gut = sem("item_gu_half_taken")
        s_gmin = sem("item_gate_clamped")
        s_sig = sem("item_exp_ready")
        s_actT = sem("item_act_half_ready")
        s_whi = sem("item_down_hi_ready")
        s_wlo = sem("item_down_lo_ready")
        s_y = sem("item_y_filled")
        s_gcur = sem("item_gate_column_ready")
        s_yrow = sem("item_y_rows_ready")
        s_sidx = sem("scatter_index_ready")
        s_scat = sem("item_rows_added")
        s_mstep = sem("item_dve_step")
        s_fss = sem("final_square_sum_ready")
        s_fout = sem("final_rows_ready")
        s_out = sem("output_stored")

        class Chain:

            def __init__(self, engine, semaphore):
                self.engine, self.sem, self.n = engine, semaphore, 0

            def inc(self, ins):
                self.n += 1
                ins.then_inc(self.sem, 1)

            def wait(self):
                self.engine.wait_ge(self.sem, self.n)

            def link(self, ins):
                self.inc(ins)
                self.wait()

        def wait_filled(eng, name):
            eng.wait_ge(s_full, plan.filled(name))

        def wait_emptied(eng, name):
            eng.wait_ge(s_act_took if plan.taker[name] == "act" else s_dve_took, plan.emptied(name))

        def cols(w, a, n=512):
            return w[0, :, a:a + n].rearrange("(k p) c -> p k c", p=P)

        def slot(s):
            return ring[:, s, :].rearrange("p (k c) -> p k c", k=KT)

        LOADS = [
            (0, cols(w_in, QS), None), (1, cols(w_in, KS), None), (2, cols(w_in, VS), None),
            (3, cols(w_in, QG), None),
            (0, cols(w_in, VG), ("qs", 3)), (1, cols(w_in, RG), ("ks", 3)),
            (2, cols(w_out, 0), ("vs", 3)), (3, cols(w_out, 512), ("kg", 3)),
            (0, cols(w_mk, 0), ("vg", 3)), (1, cols(w_mk, 512), ("rg", 3)),
            (2, cols(w_mv, 0), ("y1", 3, 0)), (3, cols(w_mv, 512), ("y1", 3, 1)),
            (0, cols(w_mq, 0), ("km", 1)), (1, cols(w_mq, 512), ("km", 3)),
            (2, cols(w_mo, 0), ("vm", 1, 0)), (3, cols(w_mo, 512), ("vm", 1, 1)),
        ]
        LOADED = [sum(s == l[0] for l in LOADS) for s in range(6)]
        SLOT_FREED = {0: ("qm", 3), 1: ("qm", 7), 2: ("y2", 3, 0), 3: ("y2", 3, 1),
                      4: ("oc", 3, 1), 5: ("oc", 3, 1)}

        def wait_slot(eng, s, nth):
            eng.wait_ge(s_w[s], 16 * nth)

        ITEM = [(0, "gate0"), (1, "lin0"), (4, "gate1"), (5, "lin1"), (2, "down0"), (3, "down1")]

        def chunk_source(e, what):
            if what == "gate0":
                return w_gu[0, e, :, 0:512].rearrange("(k p) c -> p k c", p=P)
            if what == "gate1":
                return w_gu[0, e, :, 512:1024].rearrange("(k p) c -> p k c", p=P)
            if what == "lin0":
                return w_gu[0, e, :, 1024:1536].rearrange("(k p) c -> p k c", p=P)
            if what == "lin1":
                return w_gu[0, e, :, 1536:2048].rearrange("(k p) c -> p k c", p=P)
            h = 0 if what == "down0" else 512
            return w_down[0, e, h:h + 512, :].rearrange("(k p) c -> p k c", p=P)

        def chunk_place(s, what):
            if what.startswith("down"):
                return ring[:, s, :].rearrange("p (k c) -> p k c", k=4)
            return slot(s)

        block = ctx.enter_context(nc.Block())

        @block.sync
        def _(sp):
            for i in range(TT):
                sp.dma_start(X[:, i, :], x[0, i * P:(i + 1) * P, :]).then_inc(s_x[i], 16)
            for s, src, after in LOADS:
                if after is not None:
                    wait_filled(sp, after)
                sp.dma_start(slot(s), src).then_inc(s_w[s], 16)
            for s, what in ITEM:
                wait_filled(sp, SLOT_FREED[s])
                sp.dma_start(chunk_place(s, what), chunk_source(0, what)).then_inc(s_w[s], 16)
            sp.wait_ge(s_items, 1)
            n = sp.value_load(n_items_i[0:1, 0:1], min_val=E, max_val=MAX_ITEMS)
            with sp.Fori(1, n) as t:
                e = sp.value_load(item_expert[0:1, bass.ds(t, 1)], min_val=0, max_val=E - 1)
                for j, (s, what) in enumerate(ITEM):
                    if j < 4:
                        sp.wait_ge(s_gu, 4 * t - 3 + j)
                    else:
                        sp.wait_ge(s_whi, 4 * t - 4 + 2 * (j - 3))
                        sp.wait_ge(s_wlo, 4 * t - 4 + 2 * (j - 3))
                    sp.dma_start(chunk_place(s, what), chunk_source(e, what)).then_inc(s_w[s], 16)
            sp.wait_ge(s_scat, 16 * n)
            for i in range(TT):
                sp.dma_start(X[:, i, :], acc_dram[i * P:(i + 1) * P, :]).then_inc(s_x[i], 16)
            for i in range(TT):
                sp.wait_ge(s_fout, i + 1)
                sp.dma_start(out[0, i * P:(i + 1) * P, :], xn[:, i, :]).then_inc(s_out, 16)
            sp.wait_ge(s_out, 16 * TT)

        @block.tensor
        def _(pe):
            mm = nc.tensor.matmul

            def begin(name):
                b = plan.before[name]
                if b is not None:
                    wait_emptied(pe, b)
                return bank(name)

            def done(last):
                last.then_inc(s_full, 1)

            def contract(dst, lhs, rhs):
                for k in range(KT):
                    last = mm(dst, lhsT=lhs(k), rhs=rhs(k), start=k == 0, stop=k == KT - 1)
                return last

            pe.wait_ge(s_const, 1)
            pe.wait_ge(s_gain, 80)
            b = begin(("gcols",))
            done(nc.tensor.transpose(b[:, 0:33], gain_rows, ident[0:33, 0:33]))

            def transpose_rows(stage, src, count):
                for k in range(KT):
                    b = begin((stage, k))
                    for i in range(TT):
                        if k == 0:
                            pe.wait_ge(s_xn, count + i + 1)
                        last = nc.tensor.transpose(b[:, i * P:(i + 1) * P],
                                                   src[:, i, k * P:(k + 1) * P], ident[:, :])
                    done(last)

            transpose_rows("hT", xn, 0)
            for k in range(KT):
                wait_emptied(pe, ("hT", k))

            for j in range(4):
                wait_slot(pe, 0, 1)
                b = begin(("qs", j))
                done(contract(b, lambda k: slot(0)[:, k, j * P:(j + 1) * P], lambda k: H[:, k, :]))
            for j in range(4):
                wait_slot(pe, 1, 1)
                b = begin(("ks", j))
                done(contract(b, lambda k: slot(1)[:, k, j * P:(j + 1) * P], lambda k: H[:, k, :]))
            pe.wait_ge(s_bgu, 16)
            b = begin(("bgu",))
            for f in range(16):
                last = nc.tensor.transpose(b[:, f * E:(f + 1) * E], bgu_rows[:, f * P:(f + 1) * P],
                                           ident[0:32, 0:32])
            done(last)
            for i in range(TT):
                wait_slot(pe, 2, 1)
                b = begin(("vs", i))
                done(contract(b, lambda k: H[:, k, i * P:(i + 1) * P], lambda k: slot(2)[:, k, :]))

            def fill(g):
                kind = g[0]
                b = begin(g)
                if kind == "qg":
                    j = g[1]
                    wait_slot(pe, 3, 1)
                    done(contract(b, lambda k: slot(3)[:, k, j * P:(j + 1) * P], lambda k: H[:, k, :]))
                elif kind == "kg":
                    i = g[1]
                    pe.wait_ge(s_small, 48)
                    contract(b[:, 0:16], lambda k: H[:, k, i * P:(i + 1) * P], lambda k: w_glr[:, k, :])
                    done(contract(b[:, 16:272], lambda k: H[:, k, i * P:(i + 1) * P],
                                  lambda k: slot(3)[:, k, 256:512]))
                elif kind == "vg":
                    i = g[1]
                    wait_slot(pe, 0, 2)
                    done(contract(b, lambda k: H[:, k, i * P:(i + 1) * P], lambda k: slot(0)[:, k, :]))
                elif kind == "rg":
                    i = g[1]
                    wait_slot(pe, 1, 2)
                    done(contract(b, lambda k: H[:, k, i * P:(i + 1) * P], lambda k: slot(1)[:, k, :]))
                elif kind == "glrT":
                    wait_emptied(pe, ("kg", 3))
                    for i in range(TT):
                        last = nc.tensor.transpose(b[:, i * P:(i + 1) * P], kg[:, i, 0:P], ident[:, :])
                    done(last)
                elif kind == "gz":
                    wait_emptied(pe, ("glrT",))
                    for u in range(2):
                        i = 2 * g[1] + u
                        last = mm(b[:, u * 256:(u + 1) * 256], lhsT=glrT[0:17, i * P:(i + 1) * P],
                                  rhs=w_gate[0:17, :], start=True, stop=True)
                    done(last)
                elif kind == "gs":
                    pe.wait_ge(s_loga, 1)
                    for u in range(2):
                        i = 2 * g[1] + u
                        last = mm(b[:, u * 256:(u + 1) * 256], lhsT=chunk_after[:, :], rhs=log_a[:, i, :],
                                  start=True, stop=True)
                    done(last)
                elif kind == "gend":
                    for j in range(2):
                        for i in range(TT):
                            last = mm(b[:, j * 8 + 2 * i:j * 8 + 2 * i + 2],
                                      lhsT=log_a[:, i, j * P:(j + 1) * P], rhs=chunk_of[:, :],
                                      start=True, stop=True)
                    done(last)
                elif kind == "U":
                    pe.wait_ge(s_kd, 1)
                    wait_emptied(pe, ("vg", 3))
                    u = g[1]
                    for ci, c in enumerate((4 * (u // 2) + u % 2, 4 * (u // 2) + u % 2 + 2)):
                        r = (c % 2) * 64
                        for h in range(4):
                            o = ci * 256 + (h // 2) * P
                            last = mm(b[(h % 2) * 64:(h % 2) * 64 + 64, o:o + P],
                                      lhsT=kd[r:r + 64, c // 2, h * 64:(h + 1) * 64],
                                      rhs=vg[r:r + 64, c // 2, h * P:(h + 1) * P], start=True, stop=True)
                    done(last)
                elif kind == "O":
                    wait_emptied(pe, ("U", 3))
                    wait_emptied(pe, ("qg", 1))
                    tp, par = g[1], g[2]
                    for u in range(2):
                        for half in range(2):
                            c = 2 * (2 * tp + u) + half
                            for hh in range(2):
                                o = (u * 2 + hh) * P
                                last = mm(b[half * 64:half * 64 + 64, o:o + P],
                                          lhsT=qg[par * 64:par * 64 + 64, hh, c * 64:(c + 1) * 64],
                                          rhs=state[par * 64:par * 64 + 64, c, hh, :],
                                          start=True, stop=True)
                    done(last)

            def sb_seg(h, i, skip=0):
                bk, col, _ = SB_SEG[i]
                n = T - (i + skip) * P
                return psum[:, 3 * (h % 2) + bk, col + skip * P:col + skip * P + n]

            def sb_scores(h):
                r, j = (h % 2) * 64, h // 2
                for i in range(TT):
                    last = mm(sb_seg(h, i), lhsT=ksT[r:r + 64, j, i * P:(i + 1) * P],
                              rhs=qsT[r:r + 64, j, i * P:T], start=SB_SEG[i][1] == 0, stop=True,
                              skip_group_check=True)
                last.then_inc(s_sbz, 1)

            def sb_suffix(h):
                pe.wait_ge(s_sbspm, h + 1)
                sp_ = sb_sp[h % 2]
                for i in range(TT):
                    for i2 in range(i, TT):
                        o = SB_SEG[i2][2]
                        last = mm(sb_seg(h, i, i2 - i), lhsT=(neg_tri if i2 == i else neg_ones)[:, :],
                                  rhs=sp_[:, o:o + T - i2 * P], start=False, stop=True,
                                  skip_group_check=True)
                last.then_inc(s_sbsuf, 1)

            def sb_out(h):
                b = begin(("av", h))
                pe.wait_ge(s_sbam, h + 1)
                r = (h % 2) * 64
                for i in range(TT):
                    o = SB_SEG[i][2]
                    last = mm(b[r:r + 64, i * P:T], lhsT=vs[:, i, h * 64:(h + 1) * 64],
                              rhs=sb_w[h % 2][:, o:o + T - i * P], start=i == 0, stop=i == TT - 1)
                done(last)

            for name in (("qs", 2), ("qs", 3), ("ks", 2), ("ks", 3), ("vs", 2), ("vs", 3)):
                wait_emptied(pe, name)
            sb_scores(0)
            sb_scores(1)
            for h in range(SB_HEADS):
                for g in FILL[2 * h]:
                    fill(g)
                sb_suffix(h)
                for g in FILL[2 * h + 1]:
                    fill(g)
                sb_out(h)
                if h + 2 < SB_HEADS:
                    pe.wait_ge(s_sba, h + 1)
                    sb_scores(h + 2)
            pe.wait_ge(s_sba, SB_HEADS)

            pe.wait_ge(s_og, 2)
            for f in range(4):
                b = begin(("gT", f))
                for i in range(TT):
                    last = nc.tensor.transpose(b[:, i * P:(i + 1) * P], og[:, i, f, :], ident[:, :])
                done(last)

            def project_out(stage, nth, order):
                for i in range(TT):
                    for half in range(2):
                        wait_slot(pe, 2 + half, nth)
                        b = begin((stage, i, half))
                        for n, f in enumerate(order):
                            last = mm(b, lhsT=MIX[:, f, i * P:(i + 1) * P], rhs=slot(2 + half)[:, f, :],
                                      start=n == 0, stop=n == KT - 1)
                        done(last)

            wait_emptied(pe, ("av", 7))
            for f in (2, 3):
                wait_emptied(pe, ("gT", f))
            project_out("y1", 2, (4, 5, 6, 7, 0, 1, 2, 3))

            pe.wait_ge(s_memn, 1)
            for kk in range(4):
                b = begin(("mT", kk))
                for u in range(2):
                    for mi in range(MT_):
                        k = 2 * kk + u
                        last = nc.tensor.transpose(b[:, u * 256 + mi * P:u * 256 + (mi + 1) * P],
                                                   mem_rows[:, mi, k * P:(k + 1) * P], ident[:, :])
                done(last)
            wait_emptied(pe, ("mT", 3))
            for c in range(4):
                wait_slot(pe, c // 2, 3)
                b = begin(("km", c))
                for u in range(2):
                    ct = 2 * c + u
                    last = contract(b[:, u * 256:(u + 1) * 256],
                                    lambda k: slot(ct // 4)[:, k, (ct % 4) * P:(ct % 4 + 1) * P],
                                    lambda k: mT[:, k, :])
                done(last)
            for mi in range(MT_):
                for half in range(2):
                    wait_slot(pe, 2 + half, 3)
                    b = begin(("vm", mi, half))
                    done(contract(b, lambda k: mT[:, k, mi * P:(mi + 1) * P],
                                  lambda k: slot(2 + half)[:, k, :]))

            transpose_rows("h2T", xn, TT)
            for k in (6, 7):
                wait_emptied(pe, ("h2T", k))
            for j in range(8):
                wait_slot(pe, j // 4, 4)
                b = begin(("qm", j))
                done(contract(b, lambda k: slot(j // 4)[:, k, (j % 4) * P:(j % 4 + 1) * P],
                              lambda k: H[:, k, :]))
            for name in (("qm", 6), ("qm", 7), ("km", 2), ("km", 3)):
                wait_emptied(pe, name)
            for i in range(TT):
                for hp in range(2):
                    b = begin(("sc", i, hp))
                    for u in range(2):
                        h = 2 * hp + u
                        for dt in range(2):
                            last = mm(b[:, u * 256:(u + 1) * 256], lhsT=qmT[:, 2 * h + dt, i * P:(i + 1) * P],
                                      rhs=kmT[:, 2 * h + dt, :], start=dt == 0, stop=dt == 1)
                    done(last)
            pe.wait_ge(s_prob, TT)
            for h in range(MEM_HEADS):
                for mt in range(MT_):
                    b = begin(("pT", h, mt))
                    for i in range(TT):
                        last = nc.tensor.transpose(b[:, i * P:(i + 1) * P],
                                                   probs[:, i, h, mt * P:(mt + 1) * P], ident[:, :])
                    done(last)
            for name in (("vm", 1, 0), ("vm", 1, 1)):
                wait_emptied(pe, name)
            for h in range(MEM_HEADS):
                for mt in range(MT_):
                    wait_emptied(pe, ("pT", h, mt))
                for dt in range(2):
                    b = begin(("oc", h, dt))
                    for mt in range(MT_):
                        o = h * 256 + dt * P
                        last = mm(b, lhsT=vm[:, mt, o:o + P], rhs=probsT[:, h, mt, :],
                                  start=mt == 0, stop=mt == 1)
                    done(last)
            for dt in range(2):
                wait_emptied(pe, ("oc", 3, dt))
            project_out("y2", 4, tuple(range(KT)))

            transpose_rows("h3T", xn, 2 * TT)
            for k in (6, 7):
                wait_emptied(pe, ("h3T", k))
            pe.wait_ge(s_route_w, 32)
            b = begin(("logitsT",))
            done(contract(b[0:E, :], lambda k: w_rt[:, k, :], lambda k: H[:, k, :]))
            wait_emptied(pe, ("logitsT",))
            b = begin(("logits",))
            for i in range(TT):
                last = nc.tensor.transpose(b[:, i * E:(i + 1) * E], logitsT[:, i * P:(i + 1) * P],
                                           ident[0:E, 0:E])
            done(last)
            pe.wait_ge(s_picks, 1)
            b = begin(("ranks",))
            for i in range(TT):
                for i2 in range(i + 1):
                    mm(b[:, i * E:(i + 1) * E], lhsT=(before if i2 == i else ones)[:, :],
                       rhs=picks[:, i2, :], start=i2 == 0, stop=i2 == i)
            for i in range(TT):
                last = mm(b[:, TT * E:(TT + 1) * E], lhsT=ones[:, :], rhs=picks[:, i, :], start=i == 0,
                          stop=i == TT - 1)
            done(last)
            b = begin(("gatesT",))
            done(nc.tensor.transpose(b[:, 0:P], gate_e.rearrange("p i e -> p (i e)"), ident[:, :]))
            wait_emptied(pe, ("gatesT",))
            pe.wait_ge(s_bd, 64)
            for i in range(TT):
                for half in range(2):
                    b = begin(("bd", i, half))
                    done(mm(b, lhsT=gate_eT[i * E:(i + 1) * E, :],
                            rhs=bdown[i * E:(i + 1) * E, half * 512:(half + 1) * 512],
                            start=True, stop=True))
            wait_emptied(pe, ("bd", 3, 1))

            def item_transpose(t):
                pe.wait_ge(s_xrow, 16 * (t + 1))
                for k in range(KT):
                    last = nc.tensor.transpose(psum[:, 4 + k // 4, (k % 4) * C:(k % 4 + 1) * C],
                                               x_rows[:, k * P:(k + 1) * P], ident[0:C, 0:C])
                last.then_inc(s_xt, 1)

            def item_up(t):
                first = isinstance(t, int)
                pe.wait_ge(s_xs, t + 1)
                for j, (s, _) in enumerate(ITEM[:4]):
                    pe.wait_ge(s_w[s], 16 * (LOADED[s] + 1 + t))
                    if not first:
                        pe.wait_ge(s_gut, 2 * t - 1 + j // 2)
                    for f in range(4):
                        for k in range(KT):
                            last = mm(psum[:, j, f * C:(f + 1) * C], lhsT=slot(s)[:, k, f * P:(f + 1) * P],
                                      rhs=xsT[:, k, :], start=k == 0, stop=k == KT - 1)
                    last.then_inc(s_gu, 1)

            def item_down(t, first=False):
                if not first:
                    pe.wait_ge(s_yrow, t)
                for fk in range(KT):
                    if fk % 4 == 0:
                        pe.wait_ge(s_actT, 2 * t + 1 + fk // 4)
                    if fk % 2 == 0:
                        pe.wait_ge(s_whi, 4 * t + fk // 2 + 1)
                        pe.wait_ge(s_wlo, 4 * t + fk // 2 + 1)
                    for n, (a, w) in enumerate(((act_hi, wd_hi), (act_hi, wd_lo), (act_lo, wd_hi))):
                        for half in range(2):
                            last = mm(psum[0:C, 6 + half, :], lhsT=a[:, fk, :],
                                      rhs=w[:, fk, half * 512:(half + 1) * 512],
                                      start=fk == 0 and n == 0, stop=fk == KT - 1 and n == 2)
                last.then_inc(s_y, 1)

            pe.wait_ge(s_items, 1)
            n = pe.value_load(n_items_i[0:1, 0:1], min_val=E, max_val=MAX_ITEMS)
            item_transpose(0)
            item_up(0)
            item_transpose(1)
            item_down(0, first=True)
            with pe.Fori(1, n) as t:
                item_up(t)
                item_transpose(t + 1)
                item_down(t)

        @block.scalar
        def _(act):
            ch = Chain(act, s_act)
            go = nc.scalar.activation
            nc.scalar.preload_act_table_set("natural_log_exp_and_others")
            for n, g in enumerate((g_mix, g_mem_q, g_mem_kv, g_ffn)):
                act.dma_start(gain_rows[n * KT:(n + 1) * KT, :],
                              g[0, :].rearrange("(k p) -> k p", p=P)).then_inc(s_gain, 16)
            act.dma_start(gain_rows[4 * KT:4 * KT + 1, :], g_gla_head[0:1, :]).then_inc(s_gain, 16)
            act.dma_start(w_glr[:, :, :], cols(w_in, GLR, 16)).then_inc(s_small, 16)
            act.dma_start(w_gate[0:16, :], w_gla_gate[0, :, :]).then_inc(s_small, 16)
            act.dma_start(w_gate[16:17, :], b_gla_gate[0:1, :]).then_inc(s_small, 16)
            act.dma_start(bgu_rows, b_gu[0, :, :]).then_inc(s_bgu, 16)

            def took(name, ins):
                assert plan.taker[name] == "act"
                ch_took[0] += 1
                assert plan.emptied(name) == ch_took[0], name
                ins.then_inc(s_act_took, 1)

            ch_took = [0]

            def power_half(dst, src, n):
                ch.link(go(dst, src, ACT.Ln, bias=eps_col[:, :], scale=1.0 / n))
                return go(dst, dst, ACT.Exp, scale=-0.5)

            def norm_rows(base, col):
                for i in range(TT):
                    base(i)
                    ch.link(go(xn[:, i, :], X[:, i, :], ACT.Square, accum_out=ssq[:, col + i:col + i + 1]))
                    ch.link(power_half(rstd[:, col + i:col + i + 1], ssq[:, col + i:col + i + 1], D))
                    go(xn[:, i, :], X[:, i, :], ACT.Copy,
                       scale=rstd[:, col + i:col + i + 1]).then_inc(s_xn, 1)

            act.wait_ge(s_const, 1)

            def x_loaded(i):
                act.wait_ge(s_x[i], 16)
            norm_rows(x_loaded, 0)

            def scaled_by_gain(name, dst, gain, k):
                wait_filled(act, name)
                took(name, go(dst, bank(name), ACT.Copy, scale=gcols[:, gain * KT + k:gain * KT + k + 1]))

            wait_emptied(act, ("gcols",))
            for k in range(1, KT, 2):
                scaled_by_gain(("hT", k), H[:, k, :], 0, k)
            for j in (1, 3):
                wait_filled(act, ("qs", j))
                took(("qs", j), go(qsT[:, j, :], bank(("qs", j)), ACT.Copy, scale=0.125))
            for j in (1, 3):
                wait_filled(act, ("ks", j))
                took(("ks", j), go(ksT[:, j, :], bank(("ks", j)), ACT.Copy))
            wait_filled(act, ("bgu",))
            took(("bgu",), go(bguT[:, :, :].rearrange("p f e -> p (f e)"), bank(("bgu",)), ACT.Copy))
            for i in (1, 3):
                wait_filled(act, ("vs", i))
                took(("vs", i), go(vs[:, i, :], bank(("vs", i)), ACT.Copy))

            def fill(g):
                if plan.taker[g] != "act" and g[0] not in ("gz", "rg", "O"):
                    return
                kind = g[0]
                if kind == "gz":
                    if g[1] == 1:
                        wait_emptied(act, g)
                        ch.link(go(KDb[:, :], log_a.rearrange("p i c -> p (i c)"), ACT.Abs))
                        ch.link(go(KDb[:, :], KDb[:, :], ACT.Exp, scale=-1.0))
                        go(KDb[:, :], KDb[:, :], ACT.Ln, bias=one_col[:, :]).then_inc(s_gzln, 1)
                    return
                wait_filled(act, g)
                b = bank(g)
                if kind == "qg":
                    took(g, go(qg[:, g[1], :], b, ACT.Copy, scale=0.125))
                elif kind == "vg":
                    took(g, go(vg[:, g[1], :], b, ACT.Copy))
                elif kind == "glrT":
                    took(g, go(glrT[0:16, :], b[0:16, :], ACT.Copy))
                elif kind == "gs":
                    took(g, go(kd[:, 2 * g[1]:2 * g[1] + 2, :].rearrange("p i c -> p (i c)"), b, ACT.Exp))
                elif kind == "gend":
                    took(g, go(decay[:, :], b[:, 0:16], ACT.Exp))
                elif kind == "rg":
                    if g[1] > 0:
                        wait_emptied(act, ("rg", g[1] - 1))
                    go(silu_t, b, ACT.Exp, scale=-1.0).then_inc(s_rgexp, 1)
                elif kind == "O":
                    tp, par = g[1], g[2]
                    for u in range(2):
                        for hh in range(2):
                            o, c = (u * 2 + hh) * P, 16 + 4 * (2 * tp + u) + 2 * hh + par
                            if (u, hh) != (0, 0) or par == 1 or tp == 1:
                                ch.wait()
                            ch.inc(go(gla_junk, b[:, o:o + P], ACT.Square, accum_out=ssq[:, c:c + 1]))
                    ch.wait()
                    act.sem_inc(s_osq, 1)
                    if par == 1:
                        cs = slice(16 + 8 * tp, 24 + 8 * tp)
                        ch.link(go(rstd[:, cs], ssq[:, cs], ACT.Ln, bias=eps_col[:, :], scale=1.0 / P))
                        go(rstd[:, cs], rstd[:, cs], ACT.Exp, scale=-0.5).then_inc(s_ogr, 1)

            def sb_log(h):
                act.wait_ge(s_sbz, h + 1)
                if h >= 2:
                    wait_filled(act, ("av", h - 2))
                b0 = 3 * (h % 2)
                w = sb_w[h % 2]
                ch.inc(go(w[:, 0:512], psum[:, b0, :], ACT.Abs))
                ch.link(go(w[:, 512:SB_COLS].rearrange("p (a b) -> p a b", a=2),
                           psum[:, b0 + 1:b0 + 3, 0:384], ACT.Abs))
                ch.link(go(w, w, ACT.Exp, scale=-1.0))
                go(w, w, ACT.Ln, bias=one_col[:, :]).then_inc(s_sbln, 1)

            def sb_exp(h):
                act.wait_ge(s_sbsuf, h + 1)
                act.wait_ge(s_sbsp, h + 1)
                b0 = 3 * (h % 2)
                w = sb_w[h % 2]
                ch.inc(go(w[:, 0:512], psum[:, b0, :], ACT.Exp))
                go(w[:, 512:SB_COLS].rearrange("p (a b) -> p a b", a=2), psum[:, b0 + 1:b0 + 3, 0:384],
                   ACT.Exp).then_inc(s_sba, 1)

            sb_log(0)
            sb_log(1)
            for h in range(SB_HEADS):
                for g in FILL[2 * h]:
                    fill(g)
                sb_exp(h)
                for g in FILL[2 * h + 1]:
                    fill(g)
                if h + 2 < SB_HEADS:
                    sb_log(h + 2)
            for f in (1, 3):
                wait_filled(act, ("gT", f))
                took(("gT", f), go(MIX[:, f, :], bank(("gT", f)), ACT.Copy, scale=gcols[:, 4 * KT:4 * KT + 1]))

            wait_filled(act, ("av", 7))
            act.dma_start(mem_rows, mem[0].rearrange("(i p) d -> p i d", p=P)).then_inc(s_mem, 16)
            wait_filled(act, ("O", 1, 1))
            act.dma_start(w_rt, w_router[0].rearrange("(k p) e -> p k e", p=P)).then_inc(s_route_w, 16)
            act.dma_start(b_rt, b_router[0, :].rearrange("(e a) -> e a", a=1)).then_inc(s_route_w, 16)
            act.wait_ge(s_mem, 16)
            wait_filled(act, ("O", 1, 1))
            for mi in range(MT_):
                ch.link(go(mem_junk, mem_rows[:, mi, :], ACT.Square, accum_out=ssq[:, 12 + mi:13 + mi]))
            ch.link(power_half(rstd[:, 12:14], ssq[:, 12:14], D))
            for mi in range(MT_):
                ins = go(mem_rows[:, mi, :], mem_rows[:, mi, :], ACT.Copy, scale=rstd[:, 12 + mi:13 + mi])
                if mi == 0:
                    ch.inc(ins)
            ins.then_inc(s_memn, 1)

            def res1(i):
                act.wait_ge(s_res, i + 1)
            norm_rows(res1, 4)
            for c in (1, 3):
                wait_filled(act, ("km", c))
                took(("km", c), go(kmT[:, 2 * c:2 * c + 2, :].rearrange("p a b -> p (a b)"),
                                   bank(("km", c)), ACT.Copy))
            for mi in range(MT_):
                wait_filled(act, ("vm", mi, 1))
                took(("vm", mi, 1), go(vm[:, mi, 512:1024], bank(("vm", mi, 1)), ACT.Copy))
            wait_filled(act, ("mT", 3))
            for q in range(TT):
                act.dma_start(bdown[q * E:(q + 1) * E, :], b_down[0]).then_inc(s_bd, 16)
            for k in range(1, KT, 2):
                scaled_by_gain(("h2T", k), H[:, k, :], 1, k)
            wait_filled(act, ("h2T", 7))
            for j in (1, 3, 5, 7):
                wait_filled(act, ("qm", j))
                took(("qm", j), go(qmT[:, j, :], bank(("qm", j)), ACT.Copy, scale=1.0 / 16.0))
            for i in range(TT):
                for hp in range(2):
                    act.wait_ge(s_smax, 2 * i + hp + 1)
                    b = bank(("sc", i, hp))
                    for u in range(2):
                        h = 2 * hp + u
                        c = 4 * i + h
                        ins = go(probs[:, i, h, :], b[:, u * 256:(u + 1) * 256], ACT.Exp,
                                 bias=neg_max[:, c:c + 1], accum_out=row_sum[:, c:c + 1])
                        if u == 0:
                            ch.inc(ins)
                    took(("sc", i, hp), ins)
            for h in range(MEM_HEADS):
                wait_filled(act, ("pT", h, 1))
                took(("pT", h, 1), go(probsT[:, h, 1, :], bank(("pT", h, 1)), ACT.Copy))
            for h in range(MEM_HEADS):
                wait_filled(act, ("oc", h, 1))
                took(("oc", h, 1), go(MIX[:, 2 * h + 1, :], bank(("oc", h, 1)), ACT.Copy))

            def res2(i):
                act.wait_ge(s_res, TT + i + 1)
            wait_filled(act, ("y2", 0, 0))
            norm_rows(res2, 8)
            for i in range(TT):
                act.wait_ge(s_xn, 2 * TT + i + 1)
                act.dma_start(rows_dram[i * P:(i + 1) * P, :], xn[:, i, :]).then_inc(s_rowsout, 16)
            for k in range(1, KT, 2):
                scaled_by_gain(("h3T", k), H[:, k, :], 3, k)

            act.wait_ge(s_negv, 1)
            for i in range(TT):
                ins = go(gate4[:, i, :], top_v[:, i, 0:K], ACT.Exp, bias=neg_v0[:, i:i + 1],
                         accum_out=gsum[:, i:i + 1])
                if i < TT - 1:
                    ch.inc(ins)
            ins.then_inc(s_gexp, 1)
            for i in range(TT):
                act.wait_ge(s_x2b, i + 1)
                act.dma_start(acc_dram[i * P:(i + 1) * P, :], X[:, i, :]).then_inc(s_accinit, 16)
            act.dma_start(g_fin, g_final.rearrange("(a d) -> a d", a=1).broadcast_to([P, D]))\
                .then_inc(s_gfin, 16)

            def item(t):
                first = isinstance(t, int)
                for half in range(2):
                    if not first and half == 0:
                        act.wait_ge(s_y, t)
                    s = ITEM[4 + half][0]
                    act.wait_ge(s_w[s], 16 * (LOADED[s] + 1 + t))
                    for u in range(2):
                        go(wd_hi[:, 4 * half + 2 * u:4 * half + 2 * u + 2, :],
                           chunk_place(s, "down")[:, 2 * u:2 * u + 2, :], ACT.Copy).then_inc(s_whi, 1)
                    act.wait_ge(s_gmin, 2 * t + 1 + half)
                    if not (first and half == 0):
                        act.wait_ge(s_actT, 2 * t + half)
                    go(sig_h, gate_h, ACT.Exp, scale=-ALPHA).then_inc(s_sig, 1)
                if not first:
                    act.wait_ge(s_yrow, t)
                go(gate_cur, table[:, bass.ds(t, 1), 1], ACT.Copy).then_inc(s_gcur, 1)
                act.wait_ge(s_gcur, t + 1)
                act.wait_ge(s_y, t + 1)
                if not first:
                    act.wait_ge(s_scat, 16 * t)
                go(y_rows.rearrange("p (a b) -> p a b", a=2), psum[0:C, 6:8, :], ACT.Copy,
                   scale=gate_cur).then_inc(s_yrow, 1)

            act.wait_ge(s_rowsout, 16 * TT)
            act.wait_ge(s_accinit, 16 * TT)
            act.wait_ge(s_items, 1)
            n = act.value_load(n_items_i[0:1, 0:1], min_val=E, max_val=MAX_ITEMS)
            item(0)
            with act.Fori(1, n) as t:
                item(t)
            for i in range(TT):
                act.wait_ge(s_x[i], 32)
                ch.link(go(xn[:, i, :], X[:, i, :], ACT.Square, accum_out=ssq[:, i:i + 1]))
                power_half(rstd[:, i:i + 1], ssq[:, i:i + 1], D).then_inc(s_fss, 1)

        @block.vector
        def _(dve):
            ch = Chain(dve, s_dve)
            v = nc.vector
            n_took = [0]

            def took(name, ins):
                assert plan.taker[name] == "dve"
                n_took[0] += 1
                assert plan.emptied(name) == n_took[0], name
                ins.then_inc(s_dve_took, 1)

            def copy_out(name, dst, scale=None):
                wait_filled(dve, name)
                if scale is None:
                    took(name, v.tensor_copy(dst, bank(name)))
                else:
                    took(name, v.tensor_scalar(dst, bank(name), scale, None, ALU.mult))

            wait_filled(dve, ("gcols",))
            took(("gcols",), v.tensor_copy(gcols[:, :], bank(("gcols",))[:, 0:33]))
            dve.wait_ge(s_dve_took, 1)
            for k in range(0, KT, 2):
                copy_out(("hT", k), H[:, k, :], gcols[:, k:k + 1])
            for j in (0, 2):
                copy_out(("qs", j), qsT[:, j, :], 0.125)
            for j in (0, 2):
                copy_out(("ks", j), ksT[:, j, :])
            for i in (0, 2):
                copy_out(("vs", i), vs[:, i, :])

            def sb_softplus(h):
                dve.wait_ge(s_sbln, h + 1)
                b0 = 3 * (h % 2)
                w, s_ = sb_w[h % 2], sb_sp[h % 2]
                ch.inc(v.scalar_tensor_tensor(s_[:, 0:512], psum[:, b0, :], 0.0, w[:, 0:512],
                                              ALU.max, ALU.add))
                v.scalar_tensor_tensor(s_[:, 512:SB_COLS].rearrange("p (a b) -> p a b", a=2),
                                       psum[:, b0 + 1:b0 + 3, 0:384], 0.0,
                                       w[:, 512:SB_COLS].rearrange("p (a b) -> p a b", a=2),
                                       ALU.max, ALU.add).then_inc(s_sbsp, 1)

            def gla_gate(tp):
                dve.wait_ge(s_dve_took, n_took[0])
                ch.wait()
                dve.wait_ge(s_ogr, tp + 1)
                for i in (2 * tp, 2 * tp + 1):
                    for h in range(4):
                        c = 16 + 4 * i + h
                        ins = v.scalar_tensor_tensor(og[:, i, h, :], og[:, i, h, :], rstd[:, c:c + 1],
                                                     rg[:, i, h * P:(h + 1) * P], ALU.mult, ALU.mult)
                        if (i % 2, h) != (1, 3):
                            ch.inc(ins)
                ins.then_inc(s_og, 1)

            def fill(g):
                if plan.taker[g] != "dve":
                    if g == ("gs", 1):
                        for j in range(2):
                            wait_emptied(dve, ("gs", j))
                        for i in range(2):
                            ins = v.tensor_tensor(kd[:, 2 * i:2 * i + 2, :], kd[:, 2 * i:2 * i + 2, :],
                                                  kg[:, 2 * i:2 * i + 2, 16:272], ALU.mult)
                            if i == 0:
                                ch.inc(ins)
                        ins.then_inc(s_kd, 1)
                    return
                kind = g[0]
                wait_filled(dve, g)
                b = bank(g)
                if kind == "O":
                    tp, par = g[1], g[2]
                    bb = b.rearrange("p (u hh d) -> p u hh d", u=2, hh=2)
                    dve.wait_ge(s_osq, 2 * tp + par + 1)
                    for u in range(2):
                        ins = v.tensor_copy(og[:, 2 * tp + u, par::2, :], bb[:, u, :, :])
                        if u == 0:
                            ch.inc(ins)
                    took(g, ins)
                    if par == 1:
                        gla_gate(tp)
                elif kind == "kg":
                    took(g, v.tensor_copy(kg[:, g[1], :], b[:, 0:272]))
                elif kind == "gz":
                    j = g[1]
                    took(g, v.tensor_copy(log_a[:, 2 * j:2 * j + 2, :].rearrange("p i c -> p (i c)"), b))
                    if j == 1:
                        la = log_a.rearrange("p i c -> p (i c)")
                        dve.wait_ge(s_gzln, 1)
                        v.scalar_tensor_tensor(la, la, 0.0, KDb[:, :], ALU.min,
                                               ALU.subtract).then_inc(s_loga, 1)
                elif kind == "U":
                    if g[1] % 2 == 0:
                        return
                    u = g[1]
                    prev = ("U", u - 1)
                    for step in range(4):
                        c = 4 * (u // 2) + step
                        bb = bank(prev if step % 2 == 0 else g)[:, (step // 2) * 256:(step // 2) * 256 + 256]
                        if c == 0:
                            wait_emptied(dve, ("gend",))
                            ins = v.tensor_copy(state[:, 0, :, :].rearrange("p j d -> p (j d)"), bb)
                        else:
                            for j in range(2):
                                ins = v.scalar_tensor_tensor(
                                    state[:, c, j, :], state[:, c - 1, j, :],
                                    decay[:, j * 8 + c:j * 8 + c + 1], bb[:, j * P:(j + 1) * P],
                                    ALU.mult, ALU.add)
                                if j == 0:
                                    ch.inc(ins)
                        if step == 2:
                            took(prev, ins)
                            dve.wait_ge(s_dve_took, n_took[0])
                            ch.wait()
                        elif step == 3:
                            took(g, ins)
                            dve.wait_ge(s_dve_took, n_took[0])
                            ch.wait()
                        else:
                            ch.link(ins)
                elif kind == "rg":
                    i = g[1]
                    dve.wait_ge(s_rgexp, i + 1)
                    ch.link(v.tensor_scalar_add(silu_t, silu_t, 1.0))
                    ch.link(v.reciprocal(silu_t, silu_t))
                    took(g, v.tensor_tensor(rg[:, i, :], b, silu_t, ALU.mult))

            sb_softplus(0)
            sb_softplus(1)
            for h in range(SB_HEADS):
                for part in range(2):
                    for g in FILL[2 * h + part]:
                        fill(g)
                r = (h % 2) * 64
                wait_filled(dve, ("av", h))
                took(("av", h), v.tensor_copy(MIX[r:r + 64, 4 + h // 2, :], bank(("av", h))[r:r + 64, :]))
                if h + 2 < SB_HEADS:
                    sb_softplus(h + 2)

            for f in (0, 2):
                copy_out(("gT", f), MIX[:, f, :], gcols[:, 4 * KT:4 * KT + 1])

            def add_residual(stage):
                for i in range(TT):
                    for half in range(2):
                        wait_filled(dve, (stage, i, half))
                        o = half * 512
                        ins = v.tensor_tensor(X[:, i, o:o + 512], X[:, i, o:o + 512],
                                              bank((stage, i, half)), ALU.add)
                        took((stage, i, half), ins)
                    dve.wait_ge(s_dve_took, n_took[0])
                    dve.sem_inc(s_res, 1)

            add_residual("y1")
            for kk in range(4):
                wait_filled(dve, ("mT", kk))
                for u in range(2):
                    k = 2 * kk + u
                    ins = v.tensor_scalar(mT[:, k, :], bank(("mT", kk))[:, u * 256:(u + 1) * 256],
                                          gcols[:, 2 * KT + k:2 * KT + k + 1], None, ALU.mult)
                    if u == 0:
                        ch.inc(ins)
                took(("mT", kk), ins)
            for c in (0, 2):
                copy_out(("km", c), kmT[:, 2 * c:2 * c + 2, :].rearrange("p a b -> p (a b)"))
            for mi in range(MT_):
                copy_out(("vm", mi, 0), vm[:, mi, 0:512])
            for k in range(0, KT, 2):
                copy_out(("h2T", k), H[:, k, :], gcols[:, KT + k:KT + k + 1])
            wait_filled(dve, ("h2T", 7))
            for j in (0, 2, 4, 6):
                copy_out(("qm", j), qmT[:, j, :], 1.0 / 16.0)

            def normalize(i):
                for hp in range(2):
                    wait_emptied(dve, ("sc", i, hp))
                ch.link(v.reciprocal(row_sum[:, 4 * i:4 * i + 4], row_sum[:, 4 * i:4 * i + 4]))
                v.tensor_tensor(probs[:, i, :, :], probs[:, i, :, :],
                                row_sum[:, 4 * i:4 * i + 4].unsqueeze(2).broadcast_to([P, 4, M]),
                                ALU.mult).then_inc(s_prob, 1)

            for i in range(TT):
                for hp in range(2):
                    wait_filled(dve, ("sc", i, hp))
                    c = 4 * i + 2 * hp
                    v.reduce_max(neg_max[:, c:c + 2],
                                 bank(("sc", i, hp)).rearrange("p (a b) -> p a b", a=2), AX.X,
                                 negate=True).then_inc(s_smax, 1)
                if i > 0:
                    normalize(i - 1)
            normalize(TT - 1)
            for h in range(MEM_HEADS):
                copy_out(("pT", h, 0), probsT[:, h, 0, :])
            for h in range(MEM_HEADS):
                copy_out(("oc", h, 0), MIX[:, 2 * h, :])
            add_residual("y2")
            for k in range(0, KT, 2):
                copy_out(("h3T", k), H[:, k, :], gcols[:, 3 * KT + k:3 * KT + k + 1])

            wait_filled(dve, ("logitsT",))
            dve.wait_ge(s_route_w, 32)
            took(("logitsT",), v.tensor_scalar(logitsT, bank(("logitsT",))[0:E, :], b_rt, None, ALU.add))
            wait_filled(dve, ("logits",))
            took(("logits",), v.tensor_copy(logits.rearrange("p i e -> p (i e)"), bank(("logits",))[:, 0:128]))
            dve.wait_ge(s_dve_took, n_took[0])
            for i in range(TT):
                ch.inc(v.max(top_v[:, i, :], logits[:, i, :]))
            ch.wait()
            v.tensor_single_scalar(neg_v0, top_v[:, :, 0], -1.0, ALU.mult).then_inc(s_negv, 1)
            for i in range(TT):
                ch.inc(v.max_index(top_i[:, i, :].bitcast(U32), top_v[:, i, :], logits[:, i, :]))
            ch.wait()
            ch.link(v.tensor_copy(top_f, top_i[:, :, 0:K].bitcast(U32)))
            dve.wait_ge(s_const, 2)
            ch.link(v.tensor_tensor(onehot, iota_e.unsqueeze(1).broadcast_to([P, 16, E]),
                                    top_f.rearrange("p i k -> p (i k)").unsqueeze(2)
                                    .broadcast_to([P, 16, E]), ALU.is_equal))
            ch.inc(v.reduce_sum(picks.rearrange("p i e -> p i e"),
                                onehot.rearrange("p (i k) e -> p i e k", i=TT), AX.X))
            dve.wait_ge(s_gexp, 1)
            ch.link(v.reciprocal(gsum, gsum))
            ch.link(v.tensor_tensor(gate4, gate4, gsum.unsqueeze(2).broadcast_to([P, TT, K]), ALU.mult))
            ch.link(v.tensor_tensor(oh_gate, onehot, gate4.rearrange("p i k -> p (i k)").unsqueeze(2)
                                    .broadcast_to([P, 16, E]), ALU.mult))
            ch.link(v.reduce_sum(gate_e, oh_gate.rearrange("p (i k) e -> p i e k", i=TT), AX.X))
            dve.sem_inc(s_picks, 1)
            wait_filled(dve, ("ranks",))
            took(("ranks",), v.tensor_copy(ranks, bank(("ranks",))[:, 0:160]))
            dve.wait_ge(s_dve_took, n_took[0])
            count = ranks[:, 128:160]
            rk = ranks[:, 0:128].rearrange("p (i e) -> p i e", i=TT)
            wait_filled(dve, ("gatesT",))
            took(("gatesT",), v.tensor_copy(gate_eT, bank(("gatesT",))[:, 0:128]))
            ch.link(v.tensor_single_scalar(over_e, count, float(C), ALU.is_gt))
            for j in range(2, OVER + 1):
                ch.link(v.scalar_tensor_tensor(over_e, count, float(C * j), over_e, ALU.is_gt, ALU.add))
            ch.link(v.tensor_tensor(over_m, earlier_e, over_e.unsqueeze(1).broadcast_to([P, E, E]), ALU.mult))
            ch.link(v.reduce_sum(over_before, over_m, AX.X))
            ch.link(v.tensor_tensor(over_upto, over_before, over_e, ALU.add))
            ch.link(v.tensor_single_scalar(block_f, rk, float(C), ALU.is_ge))
            for j in range(2, OVER + 1):
                ch.link(v.scalar_tensor_tensor(block_f, rk, float(C * j), block_f, ALU.is_ge, ALU.add))
            ch.link(v.scalar_tensor_tensor(slot_f, block_f, float(-C), rk, ALU.mult, ALU.add))
            ch.link(v.tensor_single_scalar(has_f, block_f, 1.0, ALU.is_ge))
            ch.link(v.tensor_tensor(item_f, block_f, over_before.unsqueeze(1).broadcast_to([P, TT, E]), ALU.add))
            ch.link(v.tensor_tensor(item_f, item_f, iota_e.unsqueeze(1).broadcast_to([P, TT, E]),
                                    ALU.subtract))
            ch.link(v.tensor_single_scalar(item_f, item_f, float(E - 1), ALU.add))
            ch.link(v.tensor_tensor(item_f, item_f, has_f, ALU.mult))
            ch.link(v.tensor_tensor(item_f, item_f, iota_e.unsqueeze(1).broadcast_to([P, TT, E]), ALU.add))
            ch.link(v.scalar_tensor_tensor(slot_f, slot_f, float(COLS), item_f, ALU.mult, ALU.add))
            for i in range(TT):
                ch.inc(v.tensor_tensor(oh_dest[:, K * i:K * i + K, :], onehot[:, K * i:K * i + K, :],
                                       slot_f[:, i, :].unsqueeze(1).broadcast_to([P, K, E]), ALU.mult))
            ch.wait()
            ch.link(v.reduce_sum(dest_f, oh_dest, AX.X))
            ch.inc(v.tensor_copy(dest_i.bitcast(I32), dest_f))
            ch.inc(v.tensor_copy(payload[:, :, 0].rearrange("p (i k) -> p i k", i=TT),
                                 tokid.unsqueeze(2).broadcast_to([P, TT, K])))
            ch.link(v.tensor_copy(payload[:, :, 1], gate4.rearrange("p i k -> p (i k)")))
            dve.sem_inc(s_pay, 1)
            ch.inc(v.tensor_copy(item_e[:, 0:E], iota_e))
            no = MAX_ITEMS - E
            ch.link(v.tensor_tensor(over_m[:, 0:no, :], over_upto.unsqueeze(1).broadcast_to([P, no, E]),
                                    iota_o[:, 0:no].unsqueeze(2).broadcast_to([P, no, E]), ALU.is_le))
            ch.link(v.reduce_sum(item_e[:, E:E + no], over_m[:, 0:no, :], AX.X))
            ch.link(v.tensor_single_scalar(n_items_f, over_upto[:, E - 1:E], float(E), ALU.add))
            ch.inc(v.tensor_copy(item_expert[:, 0:MAX_ITEMS], item_e[:, 0:MAX_ITEMS]))
            ch.link(v.tensor_copy(n_items_i, n_items_f))
            for i in range(TT):
                for half in range(2):
                    wait_filled(dve, ("bd", i, half))
                    o = half * 512
                    took(("bd", i, half), v.tensor_tensor(X[:, i, o:o + 512], X[:, i, o:o + 512],
                                                          bank(("bd", i, half)), ALU.add))
                dve.wait_ge(s_dve_took, n_took[0])
                dve.sem_inc(s_x2b, 1)
            dve.wait_ge(s_tabl, 16)
            ch.inc(v.tensor_copy(acc_row, table[:, :, 0]))
            ch.link(v.tensor_scalar_min(src_f, table[:, :, 0], float(T - 1)))
            ch.link(v.tensor_copy(src_row, src_f))
            dve.sem_inc(s_items, 1)

            PER_ITEM = 16

            def item(t):
                first = isinstance(t, int)
                steps = [0]

                def link(ins):
                    steps[0] += 1
                    ins.then_inc(s_mstep, 1)
                    dve.wait_ge(s_mstep, PER_ITEM * t + steps[0])

                e = 0 if first else dve.value_load(item_expert[0:1, bass.ds(t, 1)], min_val=0, max_val=E - 1)
                dve.wait_ge(s_xt, t + 1)
                gb = gcols[:, 3 * KT:4 * KT]
                for u in range(2):
                    ins = v.tensor_tensor(xsT[:, 4 * u:4 * u + 4, :],
                                          psum[:, 4 + u, 0:4 * C].rearrange("p (k c) -> p k c", k=4),
                                          gb[:, 4 * u:4 * u + 4].unsqueeze(2).broadcast_to([P, 4, C]),
                                          ALU.mult)
                    if u == 0:
                        steps[0] += 1
                        ins.then_inc(s_mstep, 1)
                ins.then_inc(s_xs, 1)
                link(v.tensor_copy(bias_cur, bguT[:, :, bass.ds(e, 1)].rearrange("p f o -> p (f o)")))
                for half in range(2):
                    gbank = psum[:, 2 * half, 0:4 * C].rearrange("p (k c) -> p k c", k=4)
                    lbank = psum[:, 2 * half + 1, 0:4 * C].rearrange("p (k c) -> p k c", k=4)
                    bg = bias_cur[:, 4 * half:4 * half + 4].unsqueeze(2).broadcast_to([P, 4, C])
                    bl = bias_cur[:, 8 + 4 * half:12 + 4 * half].unsqueeze(2).broadcast_to([P, 4, C])
                    s = ITEM[4 + half][0]
                    for u in range(2):
                        dve.wait_ge(s_whi, 4 * t + 2 * half + u + 1)
                        k = 4 * half + 2 * u
                        v.tensor_tensor(wd_lo[:, k:k + 2, :], chunk_place(s, "down")[:, 2 * u:2 * u + 2, :],
                                        wd_hi[:, k:k + 2, :].bitcast(F32), ALU.subtract)\
                            .then_inc(s_wlo, 1)
                    dve.wait_ge(s_gu, 4 * t + 2 * half + 1)
                    link(v.tensor_tensor(gate_h, gbank, bg, ALU.add))
                    v.tensor_scalar_min(gate_h, gate_h, LIMIT).then_inc(s_gmin, 1)
                    dve.wait_ge(s_gu, 4 * t + 2 * half + 2)
                    v.tensor_tensor(lin_h, lbank, bl, ALU.add).then_inc(s_gut, 1)
                    dve.wait_ge(s_gut, 2 * t + half + 1)
                    link(v.tensor_scalar(lin_h, lin_h, LIMIT, -LIMIT, ALU.min, ALU.max))
                    dve.wait_ge(s_sig, 2 * t + half + 1)
                    link(v.tensor_scalar_add(sig_h, sig_h, 1.0))
                    link(v.reciprocal(sig_h, sig_h))
                    link(v.tensor_tensor(gate_h, gate_h, sig_h, ALU.mult))
                    hi, lo = (a[:, 4 * half:4 * half + 4, :] for a in (act_hi, act_lo))
                    link(v.scalar_tensor_tensor(act_f, lin_h, 1.0, gate_h, ALU.add, ALU.mult))
                    link(v.tensor_copy(hi, act_f))
                    v.tensor_tensor(lo, act_f, hi.bitcast(F32), ALU.subtract).then_inc(s_actT, 1)
                    dve.wait_ge(s_actT, 2 * t + half + 1)
                assert steps[0] <= PER_ITEM
                while steps[0] < PER_ITEM:
                    steps[0] += 1
                    dve.sem_inc(s_mstep, 1)

            n = dve.value_load(n_items_i[0:1, 0:1], min_val=E, max_val=MAX_ITEMS)
            item(0)
            with dve.Fori(1, n) as t:
                item(t)
            dve.wait_ge(s_gfin, 16)
            for i in range(TT):
                dve.wait_ge(s_fss, i + 1)
                v.scalar_tensor_tensor(xn[:, i, :], X[:, i, :], rstd[:, i:i + 1], g_fin, ALU.mult,
                                       ALU.mult).then_inc(s_fout, 1)

        @block.gpsimd
        def _(pool):
            ch = Chain(pool, s_pool)
            g = nc.gpsimd
            for tile, value in ((ident, 1.0), (neg_tri, -1.0), (chunk_after, 1.0 / TAU), (before, 1.0)):
                ch.inc(g.memset(tile[:, :], value))
            ch.inc(g.memset(neg_ones[:, :], -1.0))
            ch.inc(g.memset(ones[:, :], 1.0))
            ch.inc(g.memset(one_col[:, :], 1.0))
            ch.inc(g.memset(eps_col[:, :], EPS))
            ch.inc(g.memset(glrT, 1.0))
            ch.inc(g.memset(chunk_of[:, :], 0.0))
            ch.wait()

            def keep(tile, cmp, cm, step, base=0):
                ch.inc(g.affine_select(out=tile, in_=tile, compare_op=cmp, fill=0.0, base=base,
                                       pattern=[[step, P]], channel_multiplier=cm))
            keep(ident[:, :], ALU.is_equal, 1, -1)
            keep(neg_tri[:, :], ALU.is_ge, 1, -1)
            keep(chunk_after[:, :], ALU.is_gt, 1, -1)
            keep(before[:, :], ALU.is_gt, -1, 1)
            ch.wait()
            ch.link(g.memset(chunk_of[0:64, 0:1], 1.0 / TAU))
            ch.link(g.memset(chunk_of[64:128, 1:2], 1.0 / TAU))
            ch.link(g.memset(chunk_after[64:128, 0:64], 0.0))
            pool.sem_inc(s_const, 1)
            ch.link(g.memset(prefill, 0.0))
            ch.link(g.iota(prefill[:, :, 0], pattern=[[0, COLS]], base=T, channel_multiplier=1,
                           allow_small_or_imprecise_dtypes=True))
            pool.dma_start(table_dram.rearrange("(p n) two -> p (n two)", p=C),
                           prefill.rearrange("p n two -> p (n two)")).then_inc(s_pref, 16)
            pool.wait_ge(s_pref, 16)

            def mask(buf):
                for i in range(TT):
                    o = SB_SEG[i][2]
                    ins = g.affine_select(out=buf[:, o:o + P], in_=buf[:, o:o + P], compare_op=ALU.is_gt,
                                          fill=0.0, base=0, pattern=[[1, P]], channel_multiplier=-1)
                    if i < TT - 1:
                        ch.inc(ins)
                return ins

            def mask_softplus(h):
                pool.wait_ge(s_sbsp, h + 1)
                mask(sb_sp[h % 2]).then_inc(s_sbspm, 1)

            mask_softplus(0)
            mask_softplus(1)
            for h in range(SB_HEADS):
                pool.wait_ge(s_sba, h + 1)
                mask(sb_w[h % 2]).then_inc(s_sbam, 1)
                if h + 2 < SB_HEADS:
                    mask_softplus(h + 2)

            wait_filled(pool, ("y2", 0, 0))
            wait_filled(pool, ("y2", 0, 0))
            imp = dict(allow_small_or_imprecise_dtypes=True)
            ch.inc(g.iota(iota_e, pattern=[[1, E]], base=0, channel_multiplier=0, **imp))
            ch.inc(g.iota(iota_o, pattern=[[1, 32]], base=0, channel_multiplier=0, **imp))
            ch.inc(g.iota(tokid, pattern=[[P, TT]], base=0, channel_multiplier=1, **imp))
            ch.link(g.memset(earlier_e, 1.0))
            ch.link(g.affine_select(out=earlier_e, in_=earlier_e, compare_op=ALU.is_gt, fill=0.0, base=0,
                                    pattern=[[1, E], [-1, E]], channel_multiplier=0))
            pool.sem_inc(s_const, 1)

            pool.wait_ge(s_pay, 1)
            for n in range(TT * K):
                g.indirect_dma_start(out=table_dram[:, :],
                                     out_offset=bass.IndirectOffsetOnAxis(dest_i[:, n:n + 1].bitcast(I32), 0),
                                     in_=payload[:, n, :], in_offset=None).then_inc(s_tab, 16)
            pool.wait_ge(s_tab, 16 * TT * K)
            pool.dma_start(table.rearrange("p n two -> p (n two)"),
                           table_dram.rearrange("(p n) two -> p (n two)", p=C)).then_inc(s_tabl, 16)
            pool.wait_ge(s_items, 1)
            n = pool.value_load(n_items_i[0:1, 0:1], min_val=E, max_val=MAX_ITEMS)

            def gather(t):
                if isinstance(t, int) and t == 0:
                    ch.link(g.tensor_copy(gather_idx, src_row[:, 0:1]))
                else:
                    pool.wait_ge(s_xt, t)
                    g.tensor_copy(gather_idx, src_row[:, bass.ds(t, 1)]).then_inc(s_gidx, 1)
                pool.wait_ge(s_rowsout, 16 * TT)
                if not (isinstance(t, int) and t == 0):
                    pool.wait_ge(s_gidx, t)
                g.indirect_dma_start(out=x_rows, out_offset=None, in_=rows_dram[:, :],
                                     in_offset=bass.IndirectOffsetOnAxis(gather_idx, 0))\
                    .then_inc(s_xrow, 16)

            def scatter(t):
                if not (isinstance(t, int) and t == 0):
                    pool.wait_ge(s_scat, 16 * t)
                g.tensor_copy(scatter_idx, acc_row[:, bass.ds(t, 1)]).then_inc(s_sidx, 1)
                pool.wait_ge(s_accinit, 16 * TT)
                pool.wait_ge(s_sidx, t + 1)
                pool.wait_ge(s_yrow, t + 1)
                g.indirect_dma_start(out=acc_dram[:, :],
                                     out_offset=bass.IndirectOffsetOnAxis(scatter_idx, 0),
                                     in_=y_rows, in_offset=None, compute_op=ALU.add).then_inc(s_scat, 16)

            gather(0)
            gather(1)
            scatter(0)
            with pool.Fori(1, n) as t:
                gather(t + 1)
                scatter(t)
            pool.wait_ge(s_scat, 16 * n)


_INS = ["x", "mem", "g_mix", "w_in", "w_gla_gate", "b_gla_gate", "g_gla_head", "w_out", "g_mem_q",
        "g_mem_kv", "w_mq", "w_mk", "w_mv", "w_mo", "g_ffn", "w_router", "b_router", "w_gu", "b_gu",
        "w_down", "b_down", "g_final"]


def kernel(**inputs):
    import concourse.bacc as bacc
    from concourse.bass_utils import run_bass_kernel_spmd

    nc = bacc.Bacc("TRN2", target_bir_lowering=False, num_devices=1)
    arrays, args = {}, []
    for name in _INS:
        a = np.ascontiguousarray(inputs[name])
        arrays[f"in_{name}"] = a
        args.append(nc.dram_tensor(f"in_{name}", a.shape, mybir.dt.from_np(a.dtype), kind="ExternalInput").ap())
    args.append(nc.dram_tensor("out", (1, T, D), F32, kind="ExternalOutput").ap())
    build(nc, *args)
    r = run_bass_kernel_spmd(nc, [arrays], core_ids=[0])
    return r.results[0]["out"]
```

```python
from contextlib import ExitStack

import numpy as np

import concourse.bass as bass
from concourse import mybir

F32 = mybir.dt.float32
F32R = mybir.dt.float32r
I32 = mybir.dt.int32
U32 = mybir.dt.uint32
ALU = mybir.AluOpType
ACT = mybir.ActivationFunctionType
AX = mybir.AxisListType

P = 128
T = 512
TT = T // P
D = 1024
KT = D // P
M = 256
MT_ = M // P
EPS = 1e-5
GLA_CHUNK = 64
N_CHUNKS = T // GLA_CHUNK
TAU = 16.0
SB_HEADS = 8
MEM_HEADS = 4
E = 32
K = 4
C = 96
OVER = T // C
MAX_ITEMS = E + T * K // C
COLS = MAX_ITEMS + 1
PADS = C
LIMIT = 7.0
ALPHA = 1.702
QG, KG, VG, GLR, RG, QS, KS, VS = 0, 256, 512, 1024, 1040, 1552, 2064, 2576


class Banks:

    def __init__(self):
        self.names, self.bank, self.taker, self.before = [], {}, {}, {}
        self.last, self.next = {}, 0

    def add(self, name, taker, pool=tuple(range(8))):
        b = pool[self.next % len(pool)]
        self.next += 1
        self.before[name] = self.last.get(b)
        self.last[b] = name
        self.names.append(name)
        self.bank[name], self.taker[name] = b, taker

    def filled(self, name):
        return self.names.index(name) + 1

    def emptied(self, name):
        n = self.names.index(name)
        return sum(self.taker[x] == self.taker[name] for x in self.names[:n + 1])


FILL = [
    [("qg", 0)], [("qg", 1), ("kg", 0)],
    [("kg", 1), ("kg", 2)], [("kg", 3), ("vg", 0)],
    [("glrT",), ("vg", 1)], [("gz", 0), ("gz", 1), ("vg", 2)],
    [("vg", 3)], [("gs", 0), ("gs", 1), ("gend",), ("rg", 0)],
    [("rg", 1), ("U", 0), ("U", 1)], [("U", 2), ("U", 3)],
    [("rg", 2), ("O", 0, 0), ("O", 0, 1)], [("rg", 3)],
    [("O", 1, 0), ("O", 1, 1)], [],
    [("gT", 0), ("gT", 1)], [("gT", 2), ("gT", 3)],
]
DVE_FILL = {"kg", "gz", "U", "gT"}


def plan_banks():
    plan = Banks()
    plan.add(("gcols",), "dve")
    for k in range(KT):
        plan.add(("hT", k), "dve")
    for j in range(4):
        plan.add(("qs", j), "act" if j % 2 else "dve")
    for j in range(4):
        plan.add(("ks", j), "act" if j % 2 else "dve")
    plan.add(("bgu",), "act")
    for i in range(TT):
        plan.add(("vs", i), "act" if i % 2 else "dve", pool=(6, 7))
    for h in range(SB_HEADS):
        for part in (0, 1):
            for g in FILL[2 * h + part]:
                plan.add(g, "dve" if g[0] in DVE_FILL else "act", pool=(6, 7))
        plan.add(("av", h), "dve", pool=(6, 7))
    for i in range(TT):
        plan.add(("y1", i, 0), "dve")
    for kk in range(4):
        plan.add(("mT", kk), "dve")
    for i in range(TT):
        plan.add(("y1", i, 1), "dve")
    for c in range(4):
        plan.add(("km", c), "act" if c % 2 else "dve")
    for mi in range(MT_):
        for half in range(2):
            plan.add(("vm", mi, half), "act" if half else "dve")
    for k in range(KT):
        plan.add(("h2T", k), "dve")
    for j in range(8):
        plan.add(("qm", j), "act" if j % 2 else "dve")
    for i in range(TT):
        for hp in range(2):
            plan.add(("sc", i, hp), "act")
    for h in range(MEM_HEADS):
        for mt in range(MT_):
            plan.add(("pT", h, mt), "act" if mt else "dve")
    for h in range(MEM_HEADS):
        for dt in range(2):
            plan.add(("oc", h, dt), "dve")
    for i in range(TT):
        for half in range(2):
            plan.add(("y2", i, half), "dve")
    for k in range(KT):
        plan.add(("h3T", k), "act" if k % 2 else "dve")
    plan.add(("logitsT",), "dve")
    plan.add(("logits",), "dve")
    plan.add(("ranks",), "dve")
    plan.add(("gatesT",), "dve")
    for i in range(TT):
        for half in range(2):
            if (i, half) == (TT - 1, 1):
                plan.add(("table",), None, pool=(7,))
            plan.add(("bd", i, half), "dve", pool=tuple(range(7)))
    return plan


SB_SEG = [(0, 0, 0), (1, 0, 512), (2, 0, 896), (2, 256, 1152)]
SB_COLS = 1280


def build(nc, x, mem, g_mix, w_in, w_gla_gate, b_gla_gate, g_gla_head, w_out, g_mem_q, g_mem_kv,
          w_mq, w_mk, w_mv, w_mo, g_ffn, w_router, b_router, w_gu, b_gu, w_down, b_down, g_final, out):
    plan = plan_banks()
    rows_dram = nc.dram_tensor("rows_scratch", [T, D], F32).ap()
    acc_dram = nc.dram_tensor("acc_scratch", [T + PADS, D], F32).ap()

    with ExitStack() as ctx:
        def sb(name, shape, dt=F32):
            return ctx.enter_context(nc.sbuf_tensor(name, shape, dt))

        def sem(name):
            return ctx.enter_context(nc.semaphore(name))

        ring = sb("ring", [P, 6, 4096])
        scratch = ring[:, 4:6, :].rearrange("p a b -> p (a b)")
        x_at = nc.sbuf_base
        ring_at = x_at - 4 * 6 * 4096
        X = sb("X", [P, TT, D])
        A = sb("A", [P, 4096])
        h_at = nc.sbuf_base
        H = sb("H", [P, KT, T])
        mix_at = nc.sbuf_base
        MIX = sb("MIX", [P, KT, T])
        v_at = nc.sbuf_base
        VSb = sb("VSb", [P, 2048])
        vg_at = nc.sbuf_base
        VGb = sb("VGb", [P, 2048])
        RGb = sb("RGb", [P, 2048])
        STb = sb("STb", [P, 2048])
        q_at = nc.sbuf_base
        QGb = sb("QGb", [P, 1024])
        KDb = sb("KDb", [P, 1024])
        glr_at = nc.sbuf_base
        w_glr = sb("w_glr", [P, KT, 16])
        w_glr_hi = sb("w_glr_hi", [P, KT, 16], F32R)
        ident = sb("ident", [P, P])
        neg_tri = sb("neg_tri", [P, P])
        neg_ones = sb("neg_ones", [P, P])
        chunk_after = sb("chunk_after", [P, P])
        before = sb("before", [P, P])
        ones = sb("ones", [P, P])
        chunk_of = sb("chunk_of", [P, 2])
        one_col = sb("one_col", [P, 1])
        eps_col = sb("eps_col", [P, 1])
        bguT = sb("bguT", [P, 16, E])
        gcols = sb("gcols", [P, 4 * KT + 1])
        w_gate = sb("w_gate", [17, 256])
        ssq = sb("ssq", [P, 32])
        rstd = sb("rstd", [P, 32])
        decay = sb("decay", [P, 16])

        xn = A[:, :].rearrange("p (i d) -> p i d", i=TT)
        gain_rows = RGb[0:4 * KT, 0:P]
        bgu_rows = MIX[0:E, 0:4, :].rearrange("p a b -> p (a b)")
        qsT = A[:, 0:2048].rearrange("p (j t) -> p j t", j=4)
        ksT = A[:, 2048:4096].rearrange("p (j t) -> p j t", j=4)
        vs = VSb[:, :].rearrange("p (i c) -> p i c", i=TT)
        sb_w = [scratch[:, 2560 * b:2560 * b + SB_COLS] for b in range(2)]
        sb_sp = [scratch[:, 2560 * b + SB_COLS:2560 * b + 2 * SB_COLS] for b in range(2)]
        kg = scratch[:, 5120:5120 + 1024].rearrange("p (i c) -> p i c", i=TT)
        log_a = scratch[:, 6208:6208 + 1024].rearrange("p (i c) -> p i c", i=TT)
        silu_t = scratch[:, 7232:7232 + 512]
        glrT = KDb[0:32, 0:512]
        kd = KDb[:, :].rearrange("p (i c) -> p i c", i=TT)
        vg = VGb[:, :].rearrange("p (i c) -> p i c", i=TT)
        og = VGb[:, :].rearrange("p (i h d) -> p i h d", i=TT, h=4)
        rg = RGb[:, :].rearrange("p (i c) -> p i c", i=TT)
        qg = QGb[:, :].rearrange("p (j t) -> p j t", j=2)
        state = STb[:, :].rearrange("p (c j d) -> p c j d", c=N_CHUNKS, j=2)
        gla_junk = MIX[:, 0, 0:P]
        mem_rows = VSb[:, :].rearrange("p (i d) -> p i d", i=MT_)
        mem_junk = STb[:, 0:D]
        kmT = RGb[:, :].rearrange("p (k m) -> p k m", k=KT)
        vm = STb[:, :].rearrange("p (i d) -> p i d", i=MT_)
        qmT = A[:, :].rearrange("p (j t) -> p j t", j=8)
        probs = scratch[:, 0:4096].rearrange("p (i h m) -> p i h m", i=TT, h=MEM_HEADS)
        probsT = scratch[:, 4096:8192].rearrange("p (h m t) -> p h m t", h=MEM_HEADS, m=MT_)
        neg_max = QGb[:, 0:16]
        row_sum = QGb[:, 16:32]
        w_rt = QGb[:, 32:32 + KT * E].rearrange("p (k e) -> p k e", k=KT)
        b_rt = QGb[0:E, 288:289]
        logitsT = STb[0:E, 0:T]
        logits = QGb[:, 320:448].rearrange("p (i e) -> p i e", i=TT)
        top_v = QGb[:, 448:480].rearrange("p (i k) -> p i k", i=TT)
        top_i = QGb[:, 480:512].rearrange("p (i k) -> p i k", i=TT)
        top_f = QGb[:, 512:528].rearrange("p (i k) -> p i k", i=TT)
        gate4 = QGb[:, 528:544].rearrange("p (i k) -> p i k", i=TT)
        pick_slot = QGb[:, 544:560]
        pick_item = QGb[:, 560:576]
        pick_row = QGb[:, 576:592]
        gsum = QGb[:, 608:612]
        tok_less = QGb[:, 612:616]
        iota_e = QGb[:, 616:648]
        iota_o = QGb[:, 648:648 + 32]
        picks = QGb[:, 680:808].rearrange("p (i e) -> p i e", i=TT)
        ranks = QGb[:, 808:968]
        neg_v0 = QGb[:, 968:972]
        pad_row = QGb[:, 972:973]
        over_e = VSb[:, 0:32]
        over_before = VSb[:, 32:64]
        over_upto = VSb[:, 64:96]
        block_f = VSb[:, 96:224].rearrange("p (i e) -> p i e", i=TT)
        slot_f = VSb[:, 224:352].rearrange("p (i e) -> p i e", i=TT)
        item_f = VSb[:, 352:480].rearrange("p (i e) -> p i e", i=TT)
        has_f = VSb[:, 480:608].rearrange("p (i e) -> p i e", i=TT)
        item_e = VSb[:, 608:608 + 64]
        n_items_f = VSb[:, 672:673]
        gate_e = VSb[:, 704:832].rearrange("p (i e) -> p i e", i=TT)
        gate_eT = VSb[:, 832:960]
        bdown = VSb[:, 1024:2048]
        onehot = VGb[:, 0:512].rearrange("p (n e) -> p n e", n=16)
        oh_gate = VGb[:, 512:1024].rearrange("p (n e) -> p n e", n=16)
        oh_slot = VGb[:, 1024:1536].rearrange("p (n e) -> p n e", n=16)
        oh_item = VGb[:, 1536:2048].rearrange("p (n e) -> p n e", n=16)
        earlier_e = RGb[:, 0:1024].rearrange("p (a b) -> p a b", a=E)
        over_m = RGb[:, 1024:2048].rearrange("p (a b) -> p a b", a=E)
        slot_gate = KDb[0:C, 0:COLS]
        acc_f = KDb[0:C, COLS:2 * COLS]
        acc_row = KDb[0:C, 108:108 + COLS].bitcast(I32)
        src_row = KDb[0:C, 164:164 + COLS].bitcast(I32)
        item_expert = KDb[:, 220:220 + 64].bitcast(I32)
        n_items_i = KDb[:, 284:285].bitcast(I32)
        gather_idx = KDb[0:C, 286:287].bitcast(I32)
        scatter_idx = KDb[0:C, 287:288].bitcast(I32)
        gate_cur = KDb[0:C, 288:289]
        bias_cur = KDb[:, 296:312]
        src_f = KDb[0:C, 320:320 + COLS]
        iota_c = KDb[:, 400:400 + C]
        x_rows = H[0:C, 0:2, :].rearrange("p a b -> p (a b)")
        y_rows = H[0:C, 2:4, :].rearrange("p a b -> p (a b)")
        g_fin = H[:, 4:6, :].rearrange("p a b -> p (a b)")
        fl = MIX[:, :, :].rearrange("p a b -> p (a b)")
        pick_rhs = fl[:, 0:32 * COLS].rearrange("p (n two m) -> p n two m", n=16, two=2)
        in_item = fl[:, 32 * COLS:48 * COLS].rearrange("p (n m) -> p n m", n=16)
        in_slot = STb[:, 512:512 + 16 * C].rearrange("p (n c) -> p n c", n=16)
        xsT = fl[:, 0:768].rearrange("p (k c) -> p k c", k=KT)
        act_f = fl[:, 768:1152].rearrange("p (k c) -> p k c", k=4)
        gate_h = fl[:, 1536:1920].rearrange("p (k c) -> p k c", k=4)
        lin_h = fl[:, 1920:2304].rearrange("p (k c) -> p k c", k=4)
        sig_h = fl[:, 2304:2688].rearrange("p (k c) -> p k c", k=4)

        ring_r = nc.alloc_sbuf_tensor_at("ring_split", [P, 6, 4096], F32R, offset=ring_at)
        H_hi = nc.alloc_sbuf_tensor_at("H_hi", [P, KT, T], F32R, offset=h_at)
        H_lo = nc.alloc_sbuf_tensor_at("H_lo", [P, KT, T], F32R, offset=x_at)
        w_glr_lo = nc.alloc_sbuf_tensor_at("w_glr_lo", [P, KT, 16], F32R, offset=glr_at)
        MIX_lo = nc.alloc_sbuf_tensor_at("MIX_lo", [P, KT, T], F32R, offset=mix_at)
        mT_hi = nc.alloc_sbuf_tensor_at("mT_hi", [P, KT, M], F32R, offset=vg_at)
        mT_lo = nc.alloc_sbuf_tensor_at("mT_lo", [P, KT, M], F32R, offset=q_at)

        wd_hi = nc.alloc_sbuf_tensor_at("wd_hi", [P, KT, D], F32R, offset=x_at)
        wd_lo = nc.alloc_sbuf_tensor_at("wd_lo", [P, KT, D], F32R, offset=v_at)
        act_hi = nc.alloc_sbuf_tensor_at("act_hi", [P, KT, C], F32R, offset=h_at + 3 * D * 4)
        act_lo = nc.alloc_sbuf_tensor_at("act_lo", [P, KT, C], F32R, offset=q_at)

        psum = ctx.enter_context(nc.psum_tensor("psum", [P, 8, 512], F32))

        def bank(name):
            return psum[:, plan.bank[name], :]

        s_const = sem("constants_built")
        s_x = [sem(f"x_tile_loaded_{i}") for i in range(TT)]
        s_gain = sem("gain_rows_loaded")
        s_ghead = sem("gla_gain_loaded")
        s_eps = sem("eps_built")
        s_r0 = sem("first_rstd_ready")
        s_bgu = sem("b_gu_rows_loaded")
        s_small = sem("gla_small_loaded")
        s_mem = sem("mem_rows_loaded")
        s_route_w = sem("router_weights_loaded")
        s_bd = sem("b_down_loaded")
        s_gfin = sem("g_final_loaded")
        s_w = [sem(f"ring_slot_loaded_{s}") for s in range(6)]
        s_chi = sem("chunk_hi_ready")
        s_clo = sem("chunk_lo_ready")
        s_ahi = sem("activation_hi_ready")
        s_alo = sem("mix_tile_lo_ready")
        s_full = sem("psum_bank_filled")
        s_act_took = sem("bank_emptied_by_act")
        s_dve_took = sem("bank_emptied_by_dve")
        s_act = sem("act_step")
        s_dve = sem("dve_step")
        s_pool = sem("pool_step")
        s_xn = sem("normed_rows_ready")
        s_res = sem("residual_tile_updated")
        s_sbz = sem("sb_scores_ready")
        s_sbln = sem("sb_log_ready")
        s_sbsp = sem("sb_softplus_ready")
        s_sbspm = sem("sb_softplus_masked")
        s_sbsuf = sem("sb_suffix_ready")
        s_sba = sem("sb_weights_ready")
        s_sbam = sem("sb_weights_masked")
        s_gzln = sem("gate_log_ready")
        s_loga = sem("log_decay_ready")
        s_kd = sem("decayed_keys_ready")
        s_rgexp = sem("silu_exp_ready")
        s_rgd = sem("silu_gate_ready")
        s_ogr = sem("gla_rstd_ready")
        s_og = sem("gla_rows_ready")
        s_memn = sem("mem_rows_normed")
        s_smax = sem("score_max_ready")
        s_prob = sem("probs_normalized")
        s_rowsout = sem("rows_stored")
        s_accinit = sem("accumulator_stored")
        s_x2b = sem("residual_with_bias_ready")
        s_negv = sem("top_value_negated")
        s_gexp = sem("gate_exp_ready")
        s_picks = sem("picks_ready")
        s_gatee = sem("gates_by_expert_ready")
        s_onehot = sem("tile_pick_onehots_ready")
        s_items = sem("items_ready")
        s_gidx = sem("gather_index_ready")
        s_xrow = sem("item_rows_gathered")
        s_xt = sem("item_rows_transposed")
        s_xs = sem("item_xT_ready")
        s_gu = sem("item_gu_bank_filled")
        s_gut = sem("item_gu_half_taken")
        s_gmin = sem("item_gate_clamped")
        s_sig = sem("item_exp_ready")
        s_actT = sem("item_act_half_ready")
        s_whi = sem("item_down_hi_ready")
        s_wlo = sem("item_down_lo_ready")
        s_y = sem("item_y_filled")
        s_gcur = sem("item_gate_column_ready")
        s_yrow = sem("item_y_rows_ready")
        s_sidx = sem("scatter_index_ready")
        s_scat = sem("item_rows_added")
        s_mstep = sem("item_dve_step")
        s_fss = sem("final_square_sum_ready")
        s_fout = sem("final_rows_ready")
        s_out = sem("output_stored")

        class Chain:

            def __init__(self, engine, semaphore):
                self.engine, self.sem, self.n = engine, semaphore, 0

            def inc(self, ins):
                self.n += 1
                ins.then_inc(self.sem, 1)

            def wait(self):
                self.engine.wait_ge(self.sem, self.n)

            def link(self, ins):
                self.inc(ins)
                self.wait()

        def wait_filled(eng, name):
            eng.wait_ge(s_full, plan.filled(name))

        def wait_emptied(eng, name):
            eng.wait_ge(s_act_took if plan.taker[name] == "act" else s_dve_took, plan.emptied(name))

        def cols(w, a, n=512):
            return w[0, :, a:a + n].rearrange("(k p) c -> p k c", p=P)

        def slot(s):
            return ring[:, s, :].rearrange("p (k c) -> p k c", k=KT)

        LOADS = [
            (0, cols(w_in, QS), None), (1, cols(w_in, KS), None), (2, cols(w_in, VS), None),
            (0, cols(w_in, QG), ("qs", 3)), (2, cols(w_in, VG), ("vs", 3)), (0, cols(w_in, RG), ("kg", 3)),
            (2, cols(w_out, 0), ("vg", 3)), (0, cols(w_out, 512), ("rg", 3)),
            (4, cols(w_mk, 0), ("av", 7)), (2, cols(w_mk, 512), ("y1", 3, 0)),
            (0, cols(w_mv, 0), ("y1", 3, 1)), (4, cols(w_mv, 512), ("km", 1)),
            (2, cols(w_mq, 0), ("km", 3)), (0, cols(w_mq, 512), ("vm", 1, 0)),
            (2, cols(w_mo, 0), ("qm", 3)), (0, cols(w_mo, 512), ("qm", 7)),
        ]
        X_AGAIN = 8
        LOADED = [sum(s == l[0] for l in LOADS) for s in range(6)]
        SLOT_FREED = {0: ("y2", 3, 1), 1: ("y2", 3, 1), 2: ("y2", 3, 0), 3: ("y2", 3, 0),
                      4: ("oc", 3, 1), 5: ("oc", 3, 1)}

        SPLITS = {
            "q": (0, 1, 4, None), "k": (1, 1, 5, None), "v": (2, 1, 3, None),
            "qg": (0, 2, 1, ("ks", 3)), "vg": (2, 2, 3, ("vs", 3)), "rg": (0, 3, 1, ("kg", 3)),
            "out0": (2, 3, 3, ("vg", 3)), "out1": (0, 4, 1, ("rg", 3)),
            "mk0": (4, 1, 5, ("av", 7)), "mk1": (2, 4, 3, ("y1", 3, 0)),
            "mv0": (0, 5, 1, ("y1", 3, 1)), "mv1": (4, 2, 5, ("km", 1)),
            "mq0": (2, 5, 3, ("km", 3)), "mq1": (0, 6, 1, ("vm", 1, 0)),
            "mo0": (2, 6, 3, ("qm", 3)), "mo1": (0, 7, 1, ("qm", 7)),
        }
        SPLIT_ORDER = list(SPLITS)

        def split_count(name, u):
            return 2 * SPLIT_ORDER.index(name) + u + 1

        def chunk_part(name, lo):
            return ring_r[:, SPLITS[name][0 if lo else 2], :].rearrange("p (k c) -> p k c", k=KT)

        HI_ORDER = ([("hT", k) for k in range(KT)] + [("glr",), ("mix", 4), ("mix", 5), ("mix", 6)]
                    + [("gT", f) for f in range(4)] + [("mix", 7)]
                    + [("mT", k) for k in range(KT)] + [("h2T", k) for k in range(KT)]
                    + [("oc", h, dt) for h in range(MEM_HEADS) for dt in range(2)])

        def hi_count(name):
            return HI_ORDER.index(name) + 1

        def wait_slot(eng, s, nth):
            eng.wait_ge(s_w[s], 16 * nth)

        ITEM = [(0, "gate0"), (1, "lin0"), (4, "gate1"), (5, "lin1"), (2, "down0"), (3, "down1")]

        def chunk_source(e, what):
            if what == "gate0":
                return w_gu[0, e, :, 0:512].rearrange("(k p) c -> p k c", p=P)
            if what == "gate1":
                return w_gu[0, e, :, 512:1024].rearrange("(k p) c -> p k c", p=P)
            if what == "lin0":
                return w_gu[0, e, :, 1024:1536].rearrange("(k p) c -> p k c", p=P)
            if what == "lin1":
                return w_gu[0, e, :, 1536:2048].rearrange("(k p) c -> p k c", p=P)
            h = 0 if what == "down0" else 512
            return w_down[0, e, h:h + 512, :].rearrange("(k p) c -> p k c", p=P)

        def chunk_place(s, what):
            if what.startswith("down"):
                return ring[:, s, :].rearrange("p (k c) -> p k c", k=4)
            return slot(s)

        block = ctx.enter_context(nc.Block())

        @block.sync
        def _(sp):
            for i in range(TT):
                sp.dma_start(X[:, i, :], x[0, i * P:(i + 1) * P, :]).then_inc(s_x[i], 16)
            for n, (s, src, after) in enumerate(LOADS):
                if n == X_AGAIN:
                    for i in range(TT):
                        wait_filled(sp, ("rg", 3))
                        sp.dma_start(X[:, i, :], x[0, i * P:(i + 1) * P, :]).then_inc(s_x[i], 16)
                if after is not None:
                    wait_filled(sp, after)
                sp.dma_start(slot(s), src).then_inc(s_w[s], 16)
            for i in range(TT):
                sp.wait_ge(s_xn, 2 * TT + i + 1)
                sp.dma_start(rows_dram[i * P:(i + 1) * P, :], xn[:, i, :]).then_inc(s_rowsout, 16)
            for s, what in ITEM:
                wait_filled(sp, SLOT_FREED[s])
                sp.dma_start(chunk_place(s, what), chunk_source(0, what)).then_inc(s_w[s], 16)
            sp.wait_ge(s_items, 1)
            n = sp.value_load(n_items_i[0:1, 0:1], min_val=E, max_val=MAX_ITEMS)
            with sp.Fori(1, n) as t:
                e = sp.value_load(item_expert[0:1, bass.ds(t, 1)], min_val=0, max_val=E - 1)
                for j, (s, what) in enumerate(ITEM):
                    if j < 4:
                        sp.wait_ge(s_gu, 4 * t - 3 + j)
                    else:
                        sp.wait_ge(s_whi, 4 * t - 4 + 2 * (j - 3))
                        sp.wait_ge(s_wlo, 4 * t - 4 + 2 * (j - 3))
                    sp.dma_start(chunk_place(s, what), chunk_source(e, what)).then_inc(s_w[s], 16)
            sp.wait_ge(s_scat, 16 * n)
            for i in range(TT):
                sp.dma_start(X[:, i, :], acc_dram[i * P:(i + 1) * P, :]).then_inc(s_x[i], 16)
            for i in range(TT):
                sp.wait_ge(s_fout, i + 1)
                sp.dma_start(out[0, i * P:(i + 1) * P, :], xn[:, i, :]).then_inc(s_out, 16)
            sp.wait_ge(s_out, 16 * TT)

        @block.tensor
        def _(pe):
            mm = nc.tensor.matmul

            def begin(name):
                b = plan.before[name]
                if b is not None:
                    wait_emptied(pe, b)
                return bank(name)

            def done(last):
                last.then_inc(s_full, 1)

            def contract_split(dst, lhs, rhs, order=range(KT), before_k=lambda n, k: None, last=True):
                for n, k in enumerate(order):
                    before_k(n, k)
                    for j, (a, b) in enumerate(((0, 0), (0, 1), (1, 0))):
                        ins = mm(dst, lhsT=lhs(a, k), rhs=rhs(b, k), start=n == 0 and j == 0,
                                 stop=n == KT - 1 and j == 2)
                return ins

            def wait_split(name):
                pe.wait_ge(s_chi, split_count(name, 1))
                pe.wait_ge(s_clo, split_count(name, 1))

            pe.wait_ge(s_const, 1)
            pe.wait_ge(s_gain, 64)
            b = begin(("gcols",))
            done(nc.tensor.transpose(b[:, 0:4 * KT], gain_rows, ident[0:4 * KT, 0:4 * KT]))

            def transpose_rows(stage, src, count, tiles_first):
                def transpose(k, i):
                    return nc.tensor.transpose(bank((stage, k))[:, i * P:(i + 1) * P],
                                               src[:, i, k * P:(k + 1) * P], ident[:, :])

                for i in range(TT - 1 if tiles_first else 0):
                    pe.wait_ge(s_xn, count + i + 1)
                    for k in range(KT):
                        if i == 0:
                            begin((stage, k))
                        transpose(k, i)
                for k in range(KT):
                    if not tiles_first:
                        begin((stage, k))
                    for i in range(TT - 1 if tiles_first else 0, TT):
                        if k == 0:
                            pe.wait_ge(s_xn, count + i + 1)
                        last = transpose(k, i)
                    done(last)

            transpose_rows("hT", xn, 0, False)
            def rows(i):
                return lambda lo, k: (H_lo if lo else H_hi)[:, k, i * P:(i + 1) * P]

            def all_rows(lo, k):
                return (H_lo if lo else H_hi)[:, k, :]

            def chunk_cols(name, a, n):
                return lambda lo, k: chunk_part(name, lo)[:, k, a:a + n]

            def first_rows(n, k):
                wait_emptied(pe, ("hT", k))
                if k % 4 == 0:
                    pe.wait_ge(s_chi, split_count("q", k // 4))
                    pe.wait_ge(s_clo, split_count("q", k // 4))

            for j in range(4):
                b = begin(("qs", j))
                if j == 0:
                    done(contract_split(b, chunk_cols("q", j * P, P), all_rows, before_k=first_rows))
                else:
                    done(contract_split(b, chunk_cols("q", j * P, P), all_rows))
            for j in range(4):
                wait_split("k")
                b = begin(("ks", j))
                done(contract_split(b, chunk_cols("k", j * P, P), all_rows))
            pe.wait_ge(s_bgu, 16)
            b = begin(("bgu",))
            for f in range(16):
                last = nc.tensor.transpose(b[:, f * E:(f + 1) * E], bgu_rows[:, f * P:(f + 1) * P],
                                           ident[0:32, 0:32])
            done(last)
            for i in range(TT):
                wait_split("v")
                b = begin(("vs", i))
                done(contract_split(b, rows(i), chunk_cols("v", 0, 512)))

            def fill(g):
                kind = g[0]
                b = begin(g)
                if kind == "qg":
                    wait_split("qg")
                    done(contract_split(b, chunk_cols("qg", g[1] * P, P), all_rows))
                elif kind == "kg":
                    done(contract_split(b[:, 0:256], rows(g[1]), chunk_cols("qg", 256, 256)))
                elif kind in ("vg", "rg"):
                    wait_split(kind)
                    done(contract_split(b, rows(g[1]), chunk_cols(kind, 0, 512)))
                elif kind == "glrT":
                    pe.wait_ge(s_alo, 1)
                    done(contract_split(b[0:16, :], lambda lo, k: (w_glr_lo if lo else w_glr_hi)[:, k, :],
                                        all_rows))
                elif kind == "gz":
                    wait_emptied(pe, ("glrT",))
                    for u in range(2):
                        i = 2 * g[1] + u
                        last = mm(b[:, u * 256:(u + 1) * 256], lhsT=glrT[0:17, i * P:(i + 1) * P],
                                  rhs=w_gate[0:17, :], start=True, stop=True)
                    done(last)
                elif kind == "gs":
                    pe.wait_ge(s_loga, 1)
                    for u in range(2):
                        i = 2 * g[1] + u
                        last = mm(b[:, u * 256:(u + 1) * 256], lhsT=chunk_after[:, :], rhs=log_a[:, i, :],
                                  start=True, stop=True)
                    done(last)
                elif kind == "gend":
                    for j in range(2):
                        for i in range(TT):
                            last = mm(b[:, j * 8 + 2 * i:j * 8 + 2 * i + 2],
                                      lhsT=log_a[:, i, j * P:(j + 1) * P], rhs=chunk_of[:, :],
                                      start=True, stop=True)
                    done(last)
                elif kind == "U":
                    pe.wait_ge(s_kd, 1)
                    wait_emptied(pe, ("vg", 3))
                    u = g[1]
                    for ci, c in enumerate((4 * (u // 2) + u % 2, 4 * (u // 2) + u % 2 + 2)):
                        r = (c % 2) * 64
                        for h in range(4):
                            o = ci * 256 + (h // 2) * P
                            last = mm(b[(h % 2) * 64:(h % 2) * 64 + 64, o:o + P],
                                      lhsT=kd[r:r + 64, c // 2, h * 64:(h + 1) * 64],
                                      rhs=vg[r:r + 64, c // 2, h * P:(h + 1) * P], start=True, stop=True)
                    done(last)
                elif kind == "O":
                    wait_emptied(pe, ("U", 3))
                    wait_emptied(pe, ("qg", 1))
                    tp, par = g[1], g[2]
                    for u in range(2):
                        for half in range(2):
                            c = 2 * (2 * tp + u) + half
                            for hh in range(2):
                                o = (u * 2 + hh) * P
                                last = mm(b[half * 64:half * 64 + 64, o:o + P],
                                          lhsT=qg[par * 64:par * 64 + 64, hh, c * 64:(c + 1) * 64],
                                          rhs=state[par * 64:par * 64 + 64, c, hh, :],
                                          start=True, stop=True)
                    done(last)

                elif kind == "gT":
                    pe.wait_ge(s_og, 2)
                    for i in range(TT):
                        last = nc.tensor.transpose(b[:, i * P:(i + 1) * P], og[:, i, g[1], :], ident[:, :])
                    done(last)

            def sb_seg(h, i, skip=0):
                bk, col, _ = SB_SEG[i]
                n = T - (i + skip) * P
                return psum[:, 3 * (h % 2) + bk, col + skip * P:col + skip * P + n]

            def sb_scores(h):
                r, j = (h % 2) * 64, h // 2
                for i in range(TT):
                    last = mm(sb_seg(h, i), lhsT=ksT[r:r + 64, j, i * P:(i + 1) * P],
                              rhs=qsT[r:r + 64, j, i * P:T], start=SB_SEG[i][1] == 0, stop=True,
                              skip_group_check=True)
                last.then_inc(s_sbz, 1)

            def sb_suffix(h):
                pe.wait_ge(s_sbspm, h + 1)
                sp_ = sb_sp[h % 2]
                for i in range(TT):
                    for i2 in range(i, TT):
                        o = SB_SEG[i2][2]
                        last = mm(sb_seg(h, i, i2 - i), lhsT=(neg_tri if i2 == i else neg_ones)[:, :],
                                  rhs=sp_[:, o:o + T - i2 * P], start=False, stop=True,
                                  skip_group_check=True)
                last.then_inc(s_sbsuf, 1)

            def sb_out(h):
                b = begin(("av", h))
                pe.wait_ge(s_sbam, h + 1)
                r = (h % 2) * 64
                for i in range(TT):
                    o = SB_SEG[i][2]
                    last = mm(b[r:r + 64, i * P:T], lhsT=vs[:, i, h * 64:(h + 1) * 64],
                              rhs=sb_w[h % 2][:, o:o + T - i * P], start=i == 0, stop=i == TT - 1)
                done(last)

            for name in (("qs", 2), ("qs", 3), ("ks", 2), ("ks", 3), ("vs", 2), ("vs", 3)):
                wait_emptied(pe, name)
            sb_scores(0)
            sb_scores(1)
            for h in range(SB_HEADS):
                for g in FILL[2 * h]:
                    fill(g)
                sb_suffix(h)
                for g in FILL[2 * h + 1]:
                    fill(g)
                sb_out(h)
                if h + 2 < SB_HEADS:
                    pe.wait_ge(s_sba, h + 1)
                    sb_scores(h + 2)
            pe.wait_ge(s_sba, SB_HEADS)

            def project_out(stage, i, half, name, order=tuple(range(KT)), before_k=lambda n, k: None):
                wait_split(name)
                b = begin((stage, i, half))
                done(contract_split(b, lambda lo, f: (MIX_lo if lo else H_hi)[:, f, i * P:(i + 1) * P],
                                    lambda lo, f: chunk_part(name, lo)[:, f, :], order, before_k))

            def mix_ready(n, f):
                if f < 4:
                    wait_emptied(pe, ("gT", f))
                else:
                    pe.wait_ge(s_ahi, hi_count(("mix", f)))
                    pe.wait_ge(s_alo, f - 2)

            MIX_ORDER = (4, 5, 6, 0, 1, 2, 3, 7)
            for i in range(TT):
                project_out("y1", i, 0, "out0", MIX_ORDER, mix_ready)

            pe.wait_ge(s_memn, 1)
            for kk in range(4):
                b = begin(("mT", kk))
                for u in range(2):
                    for mi in range(MT_):
                        k = 2 * kk + u
                        last = nc.tensor.transpose(b[:, u * 256 + mi * P:u * 256 + (mi + 1) * P],
                                                   mem_rows[:, mi, k * P:(k + 1) * P], ident[:, :])
                done(last)
            for i in range(TT):
                project_out("y1", i, 1, "out1", MIX_ORDER)

            def mem_part(lo):
                return mT_lo if lo else mT_hi

            wait_emptied(pe, ("mT", 3))
            for c in range(4):
                name = ("mk0", "mk1")[c // 2]
                wait_split(name)
                b = begin(("km", c))
                for u in range(2):
                    ct = (2 * c + u) % 4
                    last = contract_split(b[:, u * 256:(u + 1) * 256],
                                          lambda lo, k: chunk_part(name, lo)[:, k, ct * P:(ct + 1) * P],
                                          lambda lo, k: mem_part(lo)[:, k, :])
                done(last)
            for mi in range(MT_):
                for half in range(2):
                    name = ("mv0", "mv1")[half]
                    wait_split(name)
                    b = begin(("vm", mi, half))
                    done(contract_split(b, lambda lo, k: mem_part(lo)[:, k, mi * P:(mi + 1) * P],
                                        lambda lo, k: chunk_part(name, lo)[:, k, :]))

            transpose_rows("h2T", xn, TT, False)
            for j in range(8):
                name = ("mq0", "mq1")[j // 4]
                wait_split(name)
                b = begin(("qm", j))
                done(contract_split(b, lambda lo, k: chunk_part(name, lo)[:, k, (j % 4) * P:(j % 4 + 1) * P],
                                    lambda lo, k: (MIX_lo if lo else H_hi)[:, k, :],
                                    before_k=lambda n, k: wait_emptied(pe, ("h2T", k))))
            for name in (("qm", 6), ("qm", 7), ("km", 2), ("km", 3)):
                wait_emptied(pe, name)
            for i in range(TT):
                for hp in range(2):
                    b = begin(("sc", i, hp))
                    for u in range(2):
                        h = 2 * hp + u
                        for dt in range(2):
                            last = mm(b[:, u * 256:(u + 1) * 256], lhsT=qmT[:, 2 * h + dt, i * P:(i + 1) * P],
                                      rhs=kmT[:, 2 * h + dt, :], start=dt == 0, stop=dt == 1)
                    done(last)
            pe.wait_ge(s_prob, TT)
            for h in range(MEM_HEADS):
                for mt in range(MT_):
                    b = begin(("pT", h, mt))
                    for i in range(TT):
                        last = nc.tensor.transpose(b[:, i * P:(i + 1) * P],
                                                   probs[:, i, h, mt * P:(mt + 1) * P], ident[:, :])
                    done(last)
            for name in (("vm", 1, 0), ("vm", 1, 1)):
                wait_emptied(pe, name)
            for h in range(MEM_HEADS):
                for mt in range(MT_):
                    wait_emptied(pe, ("pT", h, mt))
                for dt in range(2):
                    b = begin(("oc", h, dt))
                    for mt in range(MT_):
                        o = h * 256 + dt * P
                        last = mm(b, lhsT=vm[:, mt, o:o + P], rhs=probsT[:, h, mt, :],
                                  start=mt == 0, stop=mt == 1)
                    done(last)
            for i in range(TT):
                for half in range(2):
                    project_out("y2", i, half, ("mo0", "mo1")[half],
                                before_k=lambda n, f: wait_emptied(pe, ("oc", f // 2, f % 2)))

            transpose_rows("h3T", xn, 2 * TT, True)
            pe.wait_ge(s_route_w, 32)
            b = begin(("logitsT",))
            for k in range(KT):
                wait_emptied(pe, ("h3T", k))
                last = mm(b[0:E, :], lhsT=w_rt[:, k, :], rhs=H[:, k, :], start=k == 0, stop=k == KT - 1)
            done(last)
            wait_emptied(pe, ("logitsT",))
            b = begin(("logits",))
            for i in range(TT):
                last = nc.tensor.transpose(b[:, i * E:(i + 1) * E], logitsT[:, i * P:(i + 1) * P],
                                           ident[0:E, 0:E])
            done(last)
            pe.wait_ge(s_picks, 1)
            b = begin(("ranks",))
            for i2 in range(TT):
                mm(b[:, i2 * E:(i2 + 1) * E], lhsT=before[:, :], rhs=picks[:, i2, :], start=i2 == 0,
                   stop=True, skip_group_check=True)
                last = mm(b[:, (i2 + 1) * E:(TT + 1) * E], lhsT=ones[:, :],
                          rhs=picks[:, i2, :].unsqueeze(1).broadcast_to([P, TT - i2, E]),
                          start=i2 == 0, stop=True, skip_group_check=True)
            done(last)
            pe.wait_ge(s_gatee, 1)
            b = begin(("gatesT",))
            done(nc.tensor.transpose(b[:, 0:P], gate_e.rearrange("p i e -> p (i e)"), ident[:, :]))
            wait_emptied(pe, ("gatesT",))
            pe.wait_ge(s_bd, 64)
            for i in range(TT):
                for half in range(2):
                    if (i, half) == (TT - 1, 1):
                        b = begin(("table",))
                        for n in range(TT * K):
                            if n % K == 0:
                                pe.wait_ge(s_onehot, n // K + 1)
                            last = mm(b[0:C, 0:2 * COLS], lhsT=in_slot[:, n, :],
                                      rhs=pick_rhs[:, n, :, :].rearrange("p two m -> p (two m)"),
                                      start=n == 0, stop=n == TT * K - 1)
                        done(last)
                    b = begin(("bd", i, half))
                    done(mm(b, lhsT=gate_eT[i * E:(i + 1) * E, :],
                            rhs=bdown[i * E:(i + 1) * E, half * 512:(half + 1) * 512],
                            start=True, stop=True))
            wait_emptied(pe, ("bd", 3, 1))

            def item_transpose(t):
                pe.wait_ge(s_xrow, 16 * (t + 1))
                for k in range(KT):
                    last = nc.tensor.transpose(psum[:, 4 + k // 4, (k % 4) * C:(k % 4 + 1) * C],
                                               x_rows[:, k * P:(k + 1) * P], ident[0:C, 0:C])
                last.then_inc(s_xt, 1)

            def item_up(t):
                first = isinstance(t, int)
                pe.wait_ge(s_xs, t + 1)
                for j, (s, _) in enumerate(ITEM[:4]):
                    pe.wait_ge(s_w[s], 16 * (LOADED[s] + 1 + t))
                    if not first:
                        pe.wait_ge(s_gut, 2 * t - 1 + j // 2)
                    for f in range(4):
                        for k in range(KT):
                            last = mm(psum[:, j, f * C:(f + 1) * C], lhsT=slot(s)[:, k, f * P:(f + 1) * P],
                                      rhs=xsT[:, k, :], start=k == 0, stop=k == KT - 1)
                    last.then_inc(s_gu, 1)

            def item_down(t, first=False):
                if not first:
                    pe.wait_ge(s_yrow, t)
                for fk in range(KT):
                    if fk % 4 == 0:
                        pe.wait_ge(s_actT, 2 * t + 1 + fk // 4)
                    if fk % 2 == 0:
                        pe.wait_ge(s_whi, 4 * t + fk // 2 + 1)
                        pe.wait_ge(s_wlo, 4 * t + fk // 2 + 1)
                    for n, (a, w) in enumerate(((act_hi, wd_hi), (act_hi, wd_lo), (act_lo, wd_hi))):
                        for half in range(2):
                            last = mm(psum[0:C, 6 + half, :], lhsT=a[:, fk, :],
                                      rhs=w[:, fk, half * 512:(half + 1) * 512],
                                      start=fk == 0 and n == 0, stop=fk == KT - 1 and n == 2)
                last.then_inc(s_y, 1)

            pe.wait_ge(s_items, 1)
            n = pe.value_load(n_items_i[0:1, 0:1], min_val=E, max_val=MAX_ITEMS)
            item_transpose(0)
            item_up(0)
            item_transpose(1)
            item_down(0, first=True)
            with pe.Fori(1, n) as t:
                item_up(t)
                item_transpose(t + 1)
                item_down(t)

        @block.scalar
        def _(act):
            ch = Chain(act, s_act)
            go = nc.scalar.activation
            nc.scalar.preload_act_table_set("natural_log_exp_and_others")
            for n, g in enumerate((g_mix, g_mem_q, g_mem_kv, g_ffn)):
                act.dma_start(gain_rows[n * KT:(n + 1) * KT, :],
                              g[0, :].rearrange("(k p) -> k p", p=P)).then_inc(s_gain, 16)

            def took(name, ins):
                assert plan.taker[name] == "act"
                ch_took[0] += 1
                assert plan.emptied(name) == ch_took[0], name
                ins.then_inc(s_act_took, 1)

            ch_took = [0]

            def power_half(dst, src, n):
                ch.link(go(dst, src, ACT.Ln, bias=eps_col[:, :], scale=1.0 / n))
                return go(dst, dst, ACT.Exp, scale=-0.5)

            def norm_rows(base, col):
                for i in range(TT):
                    base(i)
                    ch.link(go(xn[:, i, :], X[:, i, :], ACT.Square, accum_out=ssq[:, col + i:col + i + 1]))
                    ch.link(power_half(rstd[:, col + i:col + i + 1], ssq[:, col + i:col + i + 1], D))
                    go(xn[:, i, :], X[:, i, :], ACT.Copy,
                       scale=rstd[:, col + i:col + i + 1]).then_inc(s_xn, 1)

            act.wait_ge(s_eps, 1)
            for i in range(TT):
                act.wait_ge(s_x[i], 16)
                ch.link(go(xn[:, i, :], X[:, i, :], ACT.Square, accum_out=ssq[:, i:i + 1]))
                power_half(rstd[:, i:i + 1], ssq[:, i:i + 1], D).then_inc(s_r0, 1)

            act.dma_start(gcols[:, 4 * KT:4 * KT + 1],
                          g_gla_head[0, :].rearrange("(p a) -> p a", a=1)).then_inc(s_ghead, 16)
            act.dma_start(w_glr[:, :, :], cols(w_in, GLR, 16)).then_inc(s_small, 16)
            act.dma_start(w_gate[0:16, :], w_gla_gate[0, :, :]).then_inc(s_small, 16)
            act.dma_start(w_gate[16:17, :], b_gla_gate[0:1, :]).then_inc(s_small, 16)
            act.dma_start(bgu_rows, b_gu[0, :, :]).then_inc(s_bgu, 16)

            def scaled_by_gain(name, dst, gain, k):
                wait_filled(act, name)
                took(name, go(dst, bank(name), ACT.Copy, scale=gcols[:, gain * KT + k:gain * KT + k + 1]))

            def split_hi(name, u):
                s, nth, _, used = SPLITS[name]
                wait_slot(act, s, nth)
                if used is not None:
                    wait_filled(act, used)
                go(chunk_part(name, 0)[:, 4 * u:4 * u + 4, :], slot(s)[:, 4 * u:4 * u + 4, :],
                   ACT.Copy).then_inc(s_chi, 1)

            def split_chunk_hi(name):
                split_hi(name, 0)
                split_hi(name, 1)

            wait_emptied(act, ("gcols",))
            for k in range(KT):
                wait_filled(act, ("hT", k))
                go(H_hi[:, k, :], bank(("hT", k)), ACT.Copy, scale=gcols[:, k:k + 1]).then_inc(s_ahi, 1)
                if k % 4 == 3:
                    split_hi("q", k // 4)
            split_chunk_hi("k")
            act.wait_ge(s_small, 48)
            go(w_glr_hi[:, :, :], w_glr[:, :, :], ACT.Copy).then_inc(s_ahi, 1)
            for j in (1, 3):
                wait_filled(act, ("qs", j))
                took(("qs", j), go(qsT[:, j, :], bank(("qs", j)), ACT.Copy, scale=0.125))
            split_chunk_hi("v")
            for j in (1, 3):
                wait_filled(act, ("ks", j))
                took(("ks", j), go(ksT[:, j, :], bank(("ks", j)), ACT.Copy))
            wait_filled(act, ("bgu",))
            took(("bgu",), go(bguT[:, :, :].rearrange("p f e -> p (f e)"), bank(("bgu",)), ACT.Copy))
            for i in (1, 3):
                if i == 3:
                    split_chunk_hi("qg")
                wait_filled(act, ("vs", i))
                took(("vs", i), go(vs[:, i, :], bank(("vs", i)), ACT.Copy))

            def fill(g):
                if g[0] == "gT":
                    act.wait_ge(s_ghead, 16)
                    wait_filled(act, g)
                    go(H_hi[:, g[1], :], bank(g), ACT.Copy, scale=gcols[:, 4 * KT:4 * KT + 1])\
                        .then_inc(s_ahi, 1)
                    return
                if plan.taker[g] != "act" and g[0] != "gz":
                    return
                kind = g[0]
                if kind == "gz":
                    if g[1] == 1:
                        wait_emptied(act, g)
                        ch.link(go(KDb[:, :], log_a.rearrange("p i c -> p (i c)"), ACT.Abs))
                        ch.link(go(KDb[:, :], KDb[:, :], ACT.Exp, scale=-1.0))
                        go(KDb[:, :], KDb[:, :], ACT.Ln, bias=one_col[:, :]).then_inc(s_gzln, 1)
                    return
                wait_filled(act, g)
                b = bank(g)
                if kind == "qg":
                    took(g, go(qg[:, g[1], :], b, ACT.Copy, scale=0.125))
                elif kind == "vg":
                    took(g, go(vg[:, g[1], :], b, ACT.Copy))
                elif kind == "glrT":
                    took(g, go(glrT[0:16, :], b[0:16, :], ACT.Copy))
                elif kind == "gs":
                    took(g, go(kd[:, 2 * g[1]:2 * g[1] + 2, :].rearrange("p i c -> p (i c)"), b, ACT.Exp))
                elif kind == "gend":
                    took(g, go(decay[:, :], b[:, 0:16], ACT.Exp))
                elif kind == "rg":
                    if g[1] > 0:
                        act.wait_ge(s_rgd, g[1])
                    go(silu_t, b, ACT.Exp, scale=-1.0).then_inc(s_rgexp, 1)
                    took(g, go(rg[:, g[1], :], b, ACT.Copy))
                elif kind == "O":
                    tp, par = g[1], g[2]
                    for u in range(2):
                        ins = go(og[:, 2 * tp + u, par::2, :],
                                 b[:, u * 256:(u + 1) * 256].rearrange("p (hh d) -> p hh d", hh=2), ACT.Copy)
                        if u == 0:
                            ch.inc(ins)
                    took(g, ins)
                    ch.wait()
                    wait_emptied(act, g)
                    for u in range(2):
                        for hh in range(2):
                            c = 16 + 4 * (2 * tp + u) + 2 * hh + par
                            ch.link(go(gla_junk, og[:, 2 * tp + u, 2 * hh + par, :], ACT.Square,
                                       accum_out=ssq[:, c:c + 1]))
                    if par == 1:
                        cs = slice(16 + 8 * tp, 24 + 8 * tp)
                        ch.link(go(rstd[:, cs], ssq[:, cs], ACT.Ln, bias=eps_col[:, :], scale=1.0 / P))
                        go(rstd[:, cs], rstd[:, cs], ACT.Exp, scale=-0.5).then_inc(s_ogr, 1)

            def sb_log(h):
                act.wait_ge(s_sbz, h + 1)
                if h >= 2:
                    wait_filled(act, ("av", h - 2))
                b0 = 3 * (h % 2)
                w = sb_w[h % 2]
                ch.inc(go(w[:, 0:512], psum[:, b0, :], ACT.Abs))
                ch.link(go(w[:, 512:SB_COLS].rearrange("p (a b) -> p a b", a=2),
                           psum[:, b0 + 1:b0 + 3, 0:384], ACT.Abs))
                ch.link(go(w, w, ACT.Exp, scale=-1.0))
                go(w, w, ACT.Ln, bias=one_col[:, :]).then_inc(s_sbln, 1)

            def sb_exp(h):
                act.wait_ge(s_sbsuf, h + 1)
                act.wait_ge(s_sbsp, h + 1)
                b0 = 3 * (h % 2)
                w = sb_w[h % 2]
                ch.inc(go(w[:, 0:512], psum[:, b0, :], ACT.Exp))
                go(w[:, 512:SB_COLS].rearrange("p (a b) -> p a b", a=2), psum[:, b0 + 1:b0 + 3, 0:384],
                   ACT.Exp).then_inc(s_sba, 1)

            def mix_hi(f):
                wait_filled(act, ("rg", 3))
                wait_emptied(act, ("av", 2 * (f - 4) + 1))
                go(H_hi[:, f, :], MIX[:, f, :], ACT.Copy).then_inc(s_ahi, 1)

            def after_log(h):
                if h == 0:
                    split_chunk_hi("vg")
                elif h == 2:
                    split_chunk_hi("rg")
                elif h == 3:
                    split_hi("out0", 0)
                elif h == 4:
                    split_hi("out0", 1)
                elif h == 5:
                    mix_hi(4)
                    mix_hi(5)
                    split_hi("out1", 0)
                elif h == 6:
                    mix_hi(6)
                    split_hi("out1", 1)

            sb_log(0)
            sb_log(1)
            for h in range(SB_HEADS):
                for g in FILL[2 * h]:
                    fill(g)
                sb_exp(h)
                for g in FILL[2 * h + 1]:
                    fill(g)
                if h + 2 < SB_HEADS:
                    sb_log(h + 2)
                after_log(h)
            mix_hi(7)

            wait_filled(act, ("av", 7))
            act.dma_start(mem_rows, mem[0].rearrange("(i p) d -> p i d", p=P)).then_inc(s_mem, 16)
            act.wait_ge(s_mem, 16)
            wait_filled(act, ("O", 1, 1))
            for mi in range(MT_):
                ch.link(go(mem_junk, mem_rows[:, mi, :], ACT.Square, accum_out=ssq[:, 12 + mi:13 + mi]))
            ch.link(power_half(rstd[:, 12:14], ssq[:, 12:14], D))
            for mi in range(MT_):
                ins = go(mem_rows[:, mi, :], mem_rows[:, mi, :], ACT.Copy, scale=rstd[:, 12 + mi:13 + mi])
                if mi == 0:
                    ch.inc(ins)
            ins.then_inc(s_memn, 1)

            def res1(i):
                act.wait_ge(s_res, i + 1)

            def km_out(c):
                wait_filled(act, ("km", c))
                took(("km", c), go(kmT[:, 2 * c:2 * c + 2, :].rearrange("p a b -> p (a b)"),
                                   bank(("km", c)), ACT.Copy))

            split_chunk_hi("mk0")
            wait_filled(act, ("mT", 0))
            for k in range(KT):
                wait_filled(act, ("mT", k // 2))
                go(mT_hi[:, k, :], bank(("mT", k // 2))[:, (k % 2) * 256:(k % 2) * 256 + 256], ACT.Copy,
                   scale=gcols[:, 2 * KT + k:2 * KT + k + 1]).then_inc(s_ahi, 1)
            split_chunk_hi("mk1")
            norm_rows(res1, 4)
            split_chunk_hi("mv0")
            km_out(1)
            split_chunk_hi("mv1")
            km_out(3)
            split_chunk_hi("mq0")
            for mi in range(MT_):
                wait_filled(act, ("vm", mi, 1))
                took(("vm", mi, 1), go(vm[:, mi, 512:1024], bank(("vm", mi, 1)), ACT.Copy))
            wait_filled(act, ("mT", 3))
            for q in range(TT):
                act.dma_start(bdown[q * E:(q + 1) * E, :], b_down[0]).then_inc(s_bd, 16)
            for k in range(KT):
                wait_filled(act, ("h2T", k))
                go(H_hi[:, k, :], bank(("h2T", k)), ACT.Copy, scale=gcols[:, KT + k:KT + k + 1])\
                    .then_inc(s_ahi, 1)
            act.dma_start(w_rt, w_router[0].rearrange("(k p) e -> p k e", p=P)).then_inc(s_route_w, 16)
            act.dma_start(b_rt, b_router[0, :].rearrange("(e a) -> e a", a=1)).then_inc(s_route_w, 16)
            split_chunk_hi("mq1")
            for j in (1, 3, 5, 7):
                wait_filled(act, ("qm", j))
                took(("qm", j), go(qmT[:, j, :], bank(("qm", j)), ACT.Copy, scale=1.0 / 16.0))
                if j == 5:
                    split_chunk_hi("mo0")
            for i in range(TT):
                for hp in range(2):
                    act.wait_ge(s_smax, 2 * i + hp + 1)
                    b = bank(("sc", i, hp))
                    for u in range(2):
                        h = 2 * hp + u
                        c = 4 * i + h
                        ins = go(probs[:, i, h, :], b[:, u * 256:(u + 1) * 256], ACT.Exp,
                                 bias=neg_max[:, c:c + 1], accum_out=row_sum[:, c:c + 1])
                        if u == 0:
                            ch.inc(ins)
                    took(("sc", i, hp), ins)
            for h in range(MEM_HEADS):
                wait_filled(act, ("pT", h, 1))
                took(("pT", h, 1), go(probsT[:, h, 1, :], bank(("pT", h, 1)), ACT.Copy))
            split_chunk_hi("mo1")
            for h in range(MEM_HEADS):
                for dt in range(2):
                    wait_filled(act, ("oc", h, dt))
                    go(H_hi[:, 2 * h + dt, :], bank(("oc", h, dt)), ACT.Copy).then_inc(s_ahi, 1)

            def res2(i):
                act.wait_ge(s_res, TT + i + 1)
            wait_filled(act, ("y2", 0, 0))
            norm_rows(res2, 8)
            for k in range(1, KT, 2):
                scaled_by_gain(("h3T", k), H[:, k, :], 3, k)

            act.wait_ge(s_negv, 1)
            for i in range(TT):
                ins = go(gate4[:, i, :], top_v[:, i, 0:K], ACT.Exp, bias=neg_v0[:, i:i + 1],
                         accum_out=gsum[:, i:i + 1])
                if i < TT - 1:
                    ch.inc(ins)
            ins.then_inc(s_gexp, 1)
            for i in range(TT):
                act.wait_ge(s_x2b, i + 1)
                act.dma_start(acc_dram[i * P:(i + 1) * P, :], X[:, i, :]).then_inc(s_accinit, 16)
            act.dma_start(g_fin, g_final.rearrange("(a d) -> a d", a=1).broadcast_to([P, D]))\
                .then_inc(s_gfin, 16)

            def item(t):
                first = isinstance(t, int)
                for half in range(2):
                    if not first and half == 0:
                        act.wait_ge(s_y, t)
                    s = ITEM[4 + half][0]
                    act.wait_ge(s_w[s], 16 * (LOADED[s] + 1 + t))
                    for u in range(2):
                        go(wd_hi[:, 4 * half + 2 * u:4 * half + 2 * u + 2, :],
                           chunk_place(s, "down")[:, 2 * u:2 * u + 2, :], ACT.Copy).then_inc(s_whi, 1)
                    act.wait_ge(s_gmin, 2 * t + 1 + half)
                    if not (first and half == 0):
                        act.wait_ge(s_actT, 2 * t + half)
                    go(sig_h, gate_h, ACT.Exp, scale=-ALPHA).then_inc(s_sig, 1)
                if not first:
                    act.wait_ge(s_yrow, t)
                go(gate_cur, slot_gate[:, bass.ds(t, 1)], ACT.Copy).then_inc(s_gcur, 1)
                act.wait_ge(s_gcur, t + 1)
                act.wait_ge(s_y, t + 1)
                if not first:
                    act.wait_ge(s_scat, 16 * t)
                go(y_rows.rearrange("p (a b) -> p a b", a=2), psum[0:C, 6:8, :], ACT.Copy,
                   scale=gate_cur).then_inc(s_yrow, 1)

            act.wait_ge(s_rowsout, 16 * TT)
            act.wait_ge(s_accinit, 16 * TT)
            act.wait_ge(s_items, 1)
            n = act.value_load(n_items_i[0:1, 0:1], min_val=E, max_val=MAX_ITEMS)
            item(0)
            with act.Fori(1, n) as t:
                item(t)
            for i in range(TT):
                act.wait_ge(s_x[i], 48)
                ch.link(go(xn[:, i, :], X[:, i, :], ACT.Square, accum_out=ssq[:, i:i + 1]))
                power_half(rstd[:, i:i + 1], ssq[:, i:i + 1], D).then_inc(s_fss, 1)

        @block.vector
        def _(dve):
            ch = Chain(dve, s_dve)
            v = nc.vector
            n_took = [0]

            def took(name, ins):
                assert plan.taker[name] == "dve"
                n_took[0] += 1
                assert plan.emptied(name) == n_took[0], name
                ins.then_inc(s_dve_took, 1)

            def copy_out(name, dst, scale=None):
                wait_filled(dve, name)
                if scale is None:
                    took(name, v.tensor_copy(dst, bank(name)))
                else:
                    took(name, v.tensor_scalar(dst, bank(name), scale, None, ALU.mult))

            for i in range(TT):
                dve.wait_ge(s_r0, i + 1)
                v.tensor_scalar(xn[:, i, :], X[:, i, :], rstd[:, i:i + 1], None, ALU.mult)\
                    .then_inc(s_xn, 1)
                if i == 2:
                    wait_filled(dve, ("gcols",))
                    took(("gcols",), v.tensor_copy(gcols[:, 0:4 * KT], bank(("gcols",))[:, 0:4 * KT]))
            dve.wait_ge(s_dve_took, 1)
            def split_lo(name, u):
                dve.wait_ge(s_chi, split_count(name, u))
                s, nth = SPLITS[name][0:2]
                wait_slot(dve, s, nth)
                ks = slice(4 * u, 4 * u + 4)
                v.tensor_tensor(chunk_part(name, 1)[:, ks, :], slot(s)[:, ks, :],
                                chunk_part(name, 0)[:, ks, :].bitcast(F32), ALU.subtract)\
                    .then_inc(s_clo, 1)

            def split_chunk_lo(name):
                split_lo(name, 0)
                split_lo(name, 1)

            def rest(dst, src, gain, hi, name):
                dve.wait_ge(s_ahi, hi_count(name))
                return v.scalar_tensor_tensor(dst, src, gain, hi.bitcast(F32), ALU.mult, ALU.subtract)

            for k in range(KT):
                wait_filled(dve, ("hT", k))
                took(("hT", k), rest(H_lo[:, k, :], bank(("hT", k)), gcols[:, k:k + 1], H_hi[:, k, :],
                                     ("hT", k)))
                if k % 4 == 3:
                    split_lo("q", k // 4)
            split_chunk_lo("k")
            dve.wait_ge(s_ahi, hi_count(("glr",)))
            v.tensor_tensor(w_glr_lo[:, :, :], w_glr[:, :, :], w_glr_hi[:, :, :].bitcast(F32),
                            ALU.subtract).then_inc(s_alo, 1)
            for j in (0, 2):
                copy_out(("qs", j), qsT[:, j, :], 0.125)
            split_chunk_lo("v")
            for j in (0, 2):
                copy_out(("ks", j), ksT[:, j, :])
            for i in (0, 2):
                if i == 2:
                    split_chunk_lo("qg")
                copy_out(("vs", i), vs[:, i, :])

            def sb_softplus(h):
                dve.wait_ge(s_sbln, h + 1)
                b0 = 3 * (h % 2)
                w, s_ = sb_w[h % 2], sb_sp[h % 2]
                ch.inc(v.scalar_tensor_tensor(s_[:, 0:512], psum[:, b0, :], 0.0, w[:, 0:512],
                                              ALU.max, ALU.add))
                v.scalar_tensor_tensor(s_[:, 512:SB_COLS].rearrange("p (a b) -> p a b", a=2),
                                       psum[:, b0 + 1:b0 + 3, 0:384], 0.0,
                                       w[:, 512:SB_COLS].rearrange("p (a b) -> p a b", a=2),
                                       ALU.max, ALU.add).then_inc(s_sbsp, 1)

            def gla_gate(tp):
                dve.wait_ge(s_ogr, tp + 1)
                dve.wait_ge(s_rgd, 2 * tp + 2)
                for i in (2 * tp, 2 * tp + 1):
                    for h in range(4):
                        c = 16 + 4 * i + h
                        ins = v.scalar_tensor_tensor(og[:, i, h, :], og[:, i, h, :], rstd[:, c:c + 1],
                                                     rg[:, i, h * P:(h + 1) * P], ALU.mult, ALU.mult)
                        if (i % 2, h) != (1, 3):
                            ch.inc(ins)
                ins.then_inc(s_og, 1)

            def fill(g):
                if plan.taker[g] != "dve":
                    if g == ("gs", 1):
                        for j in range(2):
                            wait_emptied(dve, ("gs", j))
                        for i in range(2):
                            ins = v.tensor_tensor(kd[:, 2 * i:2 * i + 2, :], kd[:, 2 * i:2 * i + 2, :],
                                                  kg[:, 2 * i:2 * i + 2, :], ALU.mult)
                            if i == 0:
                                ch.inc(ins)
                        ins.then_inc(s_kd, 1)
                    elif g[0] == "rg":
                        i = g[1]
                        dve.wait_ge(s_rgexp, i + 1)
                        ch.link(v.tensor_scalar_add(silu_t, silu_t, 1.0))
                        ch.link(v.reciprocal(silu_t, silu_t))
                        wait_emptied(dve, g)
                        v.tensor_tensor(rg[:, i, :], rg[:, i, :], silu_t, ALU.mult).then_inc(s_rgd, 1)
                    elif g[0] == "O" and g[2] == 1:
                        gla_gate(g[1])
                    return
                kind = g[0]
                wait_filled(dve, g)
                b = bank(g)
                if kind == "gT":
                    dve.wait_ge(s_ghead, 16)
                    took(g, rest(MIX_lo[:, g[1], :], b, gcols[:, 4 * KT:4 * KT + 1], H_hi[:, g[1], :], g))
                elif kind == "kg":
                    took(g, v.tensor_copy(kg[:, g[1], :], b[:, 0:256]))
                elif kind == "gz":
                    j = g[1]
                    took(g, v.tensor_copy(log_a[:, 2 * j:2 * j + 2, :].rearrange("p i c -> p (i c)"), b))
                    if j == 1:
                        la = log_a.rearrange("p i c -> p (i c)")
                        dve.wait_ge(s_gzln, 1)
                        v.scalar_tensor_tensor(la, la, 0.0, KDb[:, :], ALU.min,
                                               ALU.subtract).then_inc(s_loga, 1)
                elif kind == "U":
                    if g[1] % 2 == 0:
                        return
                    u = g[1]
                    prev = ("U", u - 1)
                    for step in range(4):
                        c = 4 * (u // 2) + step
                        bb = bank(prev if step % 2 == 0 else g)[:, (step // 2) * 256:(step // 2) * 256 + 256]
                        if c == 0:
                            wait_emptied(dve, ("gend",))
                            ins = v.tensor_copy(state[:, 0, :, :].rearrange("p j d -> p (j d)"), bb)
                        else:
                            for j in range(2):
                                ins = v.scalar_tensor_tensor(
                                    state[:, c, j, :], state[:, c - 1, j, :],
                                    decay[:, j * 8 + c:j * 8 + c + 1], bb[:, j * P:(j + 1) * P],
                                    ALU.mult, ALU.add)
                                if j == 0:
                                    ch.inc(ins)
                        if step == 2:
                            took(prev, ins)
                            dve.wait_ge(s_dve_took, n_took[0])
                            ch.wait()
                        elif step == 3:
                            took(g, ins)
                            dve.wait_ge(s_dve_took, n_took[0])
                            ch.wait()
                        else:
                            ch.link(ins)

            def mix_lo(f):
                dve.wait_ge(s_ahi, hi_count(("mix", f)))
                v.tensor_tensor(MIX_lo[:, f, :], MIX[:, f, :], H_hi[:, f, :].bitcast(F32),
                                ALU.subtract).then_inc(s_alo, 1)

            def after_softplus(h):
                if h == 0:
                    split_chunk_lo("vg")
                elif h == 2:
                    split_chunk_lo("rg")
                elif h == 3:
                    split_lo("out0", 0)
                elif h == 4:
                    split_lo("out0", 1)
                elif h == 5:
                    mix_lo(4)
                    mix_lo(5)
                    split_lo("out1", 0)
                elif h == 6:
                    mix_lo(6)
                    split_lo("out1", 1)

            sb_softplus(0)
            sb_softplus(1)
            for h in range(SB_HEADS):
                for part in range(2):
                    for g in FILL[2 * h + part]:
                        fill(g)
                r = (h % 2) * 64
                wait_filled(dve, ("av", h))
                took(("av", h), v.tensor_copy(MIX[r:r + 64, 4 + h // 2, :], bank(("av", h))[r:r + 64, :]))
                if h + 2 < SB_HEADS:
                    sb_softplus(h + 2)
                after_softplus(h)

            mix_lo(7)

            def add_residual(stage, i, half):
                wait_filled(dve, (stage, i, half))
                dve.wait_ge(s_x[i], 32)
                o = half * 512
                took((stage, i, half), v.tensor_tensor(X[:, i, o:o + 512], X[:, i, o:o + 512],
                                                       bank((stage, i, half)), ALU.add))
                if half == 1:
                    dve.wait_ge(s_dve_took, n_took[0])
                    dve.sem_inc(s_res, 1)

            def km_out(c):
                copy_out(("km", c), kmT[:, 2 * c:2 * c + 2, :].rearrange("p a b -> p (a b)"))

            for i in range(TT):
                add_residual("y1", i, 0)
            split_chunk_lo("mk0")
            for kk in range(4):
                wait_filled(dve, ("mT", kk))
                dve.wait_ge(s_ahi, hi_count(("mT", 2 * kk + 1)))
                for u in range(2):
                    k = 2 * kk + u
                    ins = rest(mT_lo[:, k, :], bank(("mT", kk))[:, u * 256:(u + 1) * 256],
                               gcols[:, 2 * KT + k:2 * KT + k + 1], mT_hi[:, k, :], ("mT", k))
                    if u == 0:
                        ch.inc(ins)
                took(("mT", kk), ins)
            for i in range(TT):
                add_residual("y1", i, 1)
            split_chunk_lo("mk1")
            km_out(0)
            split_chunk_lo("mv0")
            km_out(2)
            split_chunk_lo("mv1")
            copy_out(("vm", 0, 0), vm[:, 0, 0:512])
            split_chunk_lo("mq0")
            copy_out(("vm", 1, 0), vm[:, 1, 0:512])
            for k in range(KT):
                wait_filled(dve, ("h2T", k))
                took(("h2T", k), rest(MIX_lo[:, k, :], bank(("h2T", k)), gcols[:, KT + k:KT + k + 1],
                                      H_hi[:, k, :], ("h2T", k)))
            split_chunk_lo("mq1")
            for j in (0, 2, 4, 6):
                copy_out(("qm", j), qmT[:, j, :], 1.0 / 16.0)
            split_chunk_lo("mo0")

            def normalize(i):
                for hp in range(2):
                    wait_emptied(dve, ("sc", i, hp))
                ch.link(v.reciprocal(row_sum[:, 4 * i:4 * i + 4], row_sum[:, 4 * i:4 * i + 4]))
                v.tensor_tensor(probs[:, i, :, :], probs[:, i, :, :],
                                row_sum[:, 4 * i:4 * i + 4].unsqueeze(2).broadcast_to([P, 4, M]),
                                ALU.mult).then_inc(s_prob, 1)

            for i in range(TT):
                for hp in range(2):
                    wait_filled(dve, ("sc", i, hp))
                    c = 4 * i + 2 * hp
                    v.reduce_max(neg_max[:, c:c + 2],
                                 bank(("sc", i, hp)).rearrange("p (a b) -> p a b", a=2), AX.X,
                                 negate=True).then_inc(s_smax, 1)
                if i > 0:
                    normalize(i - 1)
            normalize(TT - 1)
            for h in range(MEM_HEADS):
                copy_out(("pT", h, 0), probsT[:, h, 0, :])
            split_chunk_lo("mo1")
            for h in range(MEM_HEADS):
                for dt in range(2):
                    wait_filled(dve, ("oc", h, dt))
                    took(("oc", h, dt), rest(MIX_lo[:, 2 * h + dt, :], bank(("oc", h, dt)), 1.0,
                                             H_hi[:, 2 * h + dt, :], ("oc", h, dt)))
            for i in range(TT):
                for half in range(2):
                    add_residual("y2", i, half)
            for k in range(0, KT, 2):
                copy_out(("h3T", k), H[:, k, :], gcols[:, 3 * KT + k:3 * KT + k + 1])

            wait_filled(dve, ("logitsT",))
            dve.wait_ge(s_route_w, 32)
            took(("logitsT",), v.tensor_scalar(logitsT, bank(("logitsT",))[0:E, :], b_rt, None, ALU.add))
            wait_filled(dve, ("logits",))
            took(("logits",), v.tensor_copy(logits.rearrange("p i e -> p (i e)"), bank(("logits",))[:, 0:128]))
            dve.wait_ge(s_dve_took, n_took[0])
            for i in range(TT):
                ch.inc(v.max(top_v[:, i, :], logits[:, i, :]))
            ch.wait()
            v.tensor_single_scalar(neg_v0, top_v[:, :, 0], -1.0, ALU.mult).then_inc(s_negv, 1)
            for i in range(TT):
                ch.inc(v.max_index(top_i[:, i, :].bitcast(U32), top_v[:, i, :], logits[:, i, :]))
            ch.wait()
            ch.link(v.tensor_copy(top_f, top_i[:, :, 0:K].bitcast(U32)))
            dve.wait_ge(s_const, 2)
            ch.link(v.tensor_tensor(onehot, iota_e.unsqueeze(1).broadcast_to([P, 16, E]),
                                    top_f.rearrange("p i k -> p (i k)").unsqueeze(2)
                                    .broadcast_to([P, 16, E]), ALU.is_equal))
            v.reduce_sum(picks, onehot.rearrange("p (i k) e -> p i e k", i=TT), AX.X).then_inc(s_picks, 1)
            dve.wait_ge(s_gexp, 1)
            ch.link(v.reciprocal(gsum, gsum))
            ch.link(v.tensor_tensor(gate4, gate4, gsum.unsqueeze(2).broadcast_to([P, TT, K]), ALU.mult))
            ch.link(v.tensor_tensor(oh_gate, onehot, gate4.rearrange("p i k -> p (i k)").unsqueeze(2)
                                    .broadcast_to([P, 16, E]), ALU.mult))
            v.reduce_sum(gate_e, oh_gate.rearrange("p (i k) e -> p i e k", i=TT), AX.X)\
                .then_inc(s_gatee, 1)
            wait_filled(dve, ("ranks",))
            took(("ranks",), v.tensor_copy(ranks, bank(("ranks",))[:, 0:160]))
            dve.wait_ge(s_dve_took, n_took[0])
            count = ranks[:, 128:160]
            rk = ranks[:, 0:128].rearrange("p (i e) -> p i e", i=TT)
            wait_filled(dve, ("gatesT",))
            took(("gatesT",), v.tensor_copy(gate_eT, bank(("gatesT",))[:, 0:128]))
            ch.link(v.tensor_single_scalar(over_e, count, float(C), ALU.is_gt))
            for j in range(2, OVER + 1):
                ch.link(v.scalar_tensor_tensor(over_e, count, float(C * j), over_e, ALU.is_gt, ALU.add))
            ch.link(v.tensor_tensor(over_m, earlier_e, over_e.unsqueeze(1).broadcast_to([P, E, E]), ALU.mult))
            ch.link(v.reduce_sum(over_before, over_m, AX.X))
            ch.link(v.tensor_tensor(over_upto, over_before, over_e, ALU.add))
            ch.link(v.tensor_single_scalar(block_f, rk, float(C), ALU.is_ge))
            for j in range(2, OVER + 1):
                ch.link(v.scalar_tensor_tensor(block_f, rk, float(C * j), block_f, ALU.is_ge, ALU.add))
            ch.link(v.scalar_tensor_tensor(slot_f, block_f, float(-C), rk, ALU.mult, ALU.add))
            ch.link(v.tensor_single_scalar(has_f, block_f, 1.0, ALU.is_ge))
            ch.link(v.tensor_tensor(item_f, block_f, over_before.unsqueeze(1).broadcast_to([P, TT, E]),
                                    ALU.add))
            ch.link(v.tensor_tensor(item_f, item_f, iota_e.unsqueeze(1).broadcast_to([P, TT, E]),
                                    ALU.subtract))
            ch.link(v.tensor_single_scalar(item_f, item_f, float(E - 1), ALU.add))
            ch.link(v.tensor_tensor(item_f, item_f, has_f, ALU.mult))
            ch.link(v.tensor_tensor(item_f, item_f, iota_e.unsqueeze(1).broadcast_to([P, TT, E]), ALU.add))
            for i in range(TT):
                tile = slice(K * i, K * i + K)
                ch.inc(v.tensor_tensor(oh_slot[:, tile, :], onehot[:, tile, :],
                                       slot_f[:, i, :].unsqueeze(1).broadcast_to([P, K, E]), ALU.mult))
                ch.inc(v.tensor_tensor(oh_item[:, tile, :], onehot[:, tile, :],
                                       item_f[:, i, :].unsqueeze(1).broadcast_to([P, K, E]), ALU.mult))
            ch.wait()
            ch.inc(v.reduce_sum(pick_slot, oh_slot, AX.X))
            ch.link(v.reduce_sum(pick_item, oh_item, AX.X))
            ch.inc(v.tensor_tensor(pick_row.rearrange("p (i k) -> p i k", i=TT),
                                   tok_less.unsqueeze(2).broadcast_to([P, TT, K]),
                                   pick_slot.rearrange("p (i k) -> p i k", i=TT), ALU.subtract))
            for i in range(TT):
                tile = slice(K * i, K * i + K)

                def over(a, n):
                    return a.unsqueeze(2).broadcast_to([P, K, n])
                ch.inc(v.tensor_tensor(in_item[:, tile, :], iota_c[:, 0:COLS].unsqueeze(1)
                                       .broadcast_to([P, K, COLS]), over(pick_item[:, tile], COLS),
                                       ALU.is_equal))
                ch.link(v.tensor_tensor(in_slot[:, tile, :], iota_c.unsqueeze(1).broadcast_to([P, K, C]),
                                        over(pick_slot[:, tile], C), ALU.is_equal))
                ch.inc(v.tensor_tensor(pick_rhs[:, tile, 0, :], in_item[:, tile, :],
                                       over(pick_row[:, tile], COLS), ALU.mult))
                v.tensor_tensor(pick_rhs[:, tile, 1, :], in_item[:, tile, :],
                                over(gate4[:, i, :], COLS), ALU.mult).then_inc(s_onehot, 1)
            ch.inc(v.tensor_copy(item_e[:, 0:E], iota_e))
            no = MAX_ITEMS - E
            ch.link(v.tensor_tensor(over_m[:, 0:no, :], over_upto.unsqueeze(1).broadcast_to([P, no, E]),
                                    iota_o[:, 0:no].unsqueeze(2).broadcast_to([P, no, E]), ALU.is_le))
            ch.link(v.reduce_sum(item_e[:, E:E + no], over_m[:, 0:no, :], AX.X))
            ch.link(v.tensor_single_scalar(n_items_f, over_upto[:, E - 1:E], float(E), ALU.add))
            ch.inc(v.tensor_copy(item_expert[:, 0:MAX_ITEMS], item_e[:, 0:MAX_ITEMS]))
            ch.link(v.tensor_copy(n_items_i, n_items_f))
            wait_filled(dve, ("table",))
            b = bank(("table",))[0:C, :]
            ch.inc(v.tensor_scalar(acc_f, b[:, 0:COLS], pad_row[0:C, :], None, ALU.add))
            ch.link(v.tensor_copy(slot_gate, b[:, COLS:2 * COLS]))
            ch.inc(v.tensor_copy(acc_row, acc_f))
            ch.link(v.tensor_scalar_min(src_f, acc_f, float(T - 1)))
            ch.link(v.tensor_copy(src_row, src_f))
            dve.sem_inc(s_items, 1)
            for i in range(TT):
                for half in range(2):
                    wait_filled(dve, ("bd", i, half))
                    o = half * 512
                    took(("bd", i, half), v.tensor_tensor(X[:, i, o:o + 512], X[:, i, o:o + 512],
                                                          bank(("bd", i, half)), ALU.add))
                dve.wait_ge(s_dve_took, n_took[0])
                dve.sem_inc(s_x2b, 1)

            PER_ITEM = 16

            def item(t):
                first = isinstance(t, int)
                steps = [0]

                def link(ins):
                    steps[0] += 1
                    ins.then_inc(s_mstep, 1)
                    dve.wait_ge(s_mstep, PER_ITEM * t + steps[0])

                e = 0 if first else dve.value_load(item_expert[0:1, bass.ds(t, 1)], min_val=0, max_val=E - 1)
                dve.wait_ge(s_xt, t + 1)
                gb = gcols[:, 3 * KT:4 * KT]
                for u in range(2):
                    ins = v.tensor_tensor(xsT[:, 4 * u:4 * u + 4, :],
                                          psum[:, 4 + u, 0:4 * C].rearrange("p (k c) -> p k c", k=4),
                                          gb[:, 4 * u:4 * u + 4].unsqueeze(2).broadcast_to([P, 4, C]),
                                          ALU.mult)
                    if u == 0:
                        steps[0] += 1
                        ins.then_inc(s_mstep, 1)
                ins.then_inc(s_xs, 1)
                link(v.tensor_copy(bias_cur, bguT[:, :, bass.ds(e, 1)].rearrange("p f o -> p (f o)")))
                for half in range(2):
                    gbank = psum[:, 2 * half, 0:4 * C].rearrange("p (k c) -> p k c", k=4)
                    lbank = psum[:, 2 * half + 1, 0:4 * C].rearrange("p (k c) -> p k c", k=4)
                    bg = bias_cur[:, 4 * half:4 * half + 4].unsqueeze(2).broadcast_to([P, 4, C])
                    bl = bias_cur[:, 8 + 4 * half:12 + 4 * half].unsqueeze(2).broadcast_to([P, 4, C])
                    s = ITEM[4 + half][0]
                    for u in range(2):
                        dve.wait_ge(s_whi, 4 * t + 2 * half + u + 1)
                        k = 4 * half + 2 * u
                        v.tensor_tensor(wd_lo[:, k:k + 2, :], chunk_place(s, "down")[:, 2 * u:2 * u + 2, :],
                                        wd_hi[:, k:k + 2, :].bitcast(F32), ALU.subtract)\
                            .then_inc(s_wlo, 1)
                    dve.wait_ge(s_gu, 4 * t + 2 * half + 1)
                    link(v.tensor_tensor(gate_h, gbank, bg, ALU.add))
                    v.tensor_scalar_min(gate_h, gate_h, LIMIT).then_inc(s_gmin, 1)
                    dve.wait_ge(s_sig, 2 * t + half + 1)
                    link(v.tensor_scalar_add(sig_h, sig_h, 1.0))
                    link(v.reciprocal(sig_h, sig_h))
                    link(v.tensor_tensor(gate_h, gate_h, sig_h, ALU.mult))
                    dve.wait_ge(s_gu, 4 * t + 2 * half + 2)
                    v.tensor_tensor(lin_h, lbank, bl, ALU.add).then_inc(s_gut, 1)
                    dve.wait_ge(s_gut, 2 * t + half + 1)
                    link(v.tensor_scalar(lin_h, lin_h, LIMIT, -LIMIT, ALU.min, ALU.max))
                    hi, lo = (a[:, 4 * half:4 * half + 4, :] for a in (act_hi, act_lo))
                    link(v.scalar_tensor_tensor(act_f, lin_h, 1.0, gate_h, ALU.add, ALU.mult))
                    link(v.tensor_copy(hi, act_f))
                    v.tensor_tensor(lo, act_f, hi.bitcast(F32), ALU.subtract).then_inc(s_actT, 1)
                    dve.wait_ge(s_actT, 2 * t + half + 1)
                assert steps[0] <= PER_ITEM
                while steps[0] < PER_ITEM:
                    steps[0] += 1
                    dve.sem_inc(s_mstep, 1)

            n = dve.value_load(n_items_i[0:1, 0:1], min_val=E, max_val=MAX_ITEMS)
            item(0)
            with dve.Fori(1, n) as t:
                item(t)
            dve.wait_ge(s_gfin, 16)
            for i in range(TT):
                dve.wait_ge(s_fss, i + 1)
                v.scalar_tensor_tensor(xn[:, i, :], X[:, i, :], rstd[:, i:i + 1], g_fin, ALU.mult,
                                       ALU.mult).then_inc(s_fout, 1)

        @block.gpsimd
        def _(pool):
            ch = Chain(pool, s_pool)
            g = nc.gpsimd
            ch.link(g.memset(eps_col[:, :], EPS))
            pool.sem_inc(s_eps, 1)
            for tile, value in ((ident, 1.0), (neg_tri, -1.0), (chunk_after, 1.0 / TAU), (before, 1.0)):
                ch.inc(g.memset(tile[:, :], value))
            ch.inc(g.memset(neg_ones[:, :], -1.0))
            ch.inc(g.memset(ones[:, :], 1.0))
            ch.inc(g.memset(one_col[:, :], 1.0))
            ch.inc(g.memset(glrT, 1.0))
            ch.inc(g.memset(chunk_of[:, :], 0.0))
            ch.wait()

            def keep(tile, cmp, cm, step, base=0):
                ch.inc(g.affine_select(out=tile, in_=tile, compare_op=cmp, fill=0.0, base=base,
                                       pattern=[[step, P]], channel_multiplier=cm))
            keep(ident[:, :], ALU.is_equal, 1, -1)
            keep(neg_tri[:, :], ALU.is_ge, 1, -1)
            keep(chunk_after[:, :], ALU.is_gt, 1, -1)
            keep(before[:, :], ALU.is_gt, -1, 1)
            ch.wait()
            ch.link(g.memset(chunk_of[0:64, 0:1], 1.0 / TAU))
            ch.link(g.memset(chunk_of[64:128, 1:2], 1.0 / TAU))
            ch.link(g.memset(chunk_after[64:128, 0:64], 0.0))
            pool.sem_inc(s_const, 1)
            def mask(buf):
                for i in range(TT):
                    o = SB_SEG[i][2]
                    ins = g.affine_select(out=buf[:, o:o + P], in_=buf[:, o:o + P], compare_op=ALU.is_gt,
                                          fill=0.0, base=0, pattern=[[1, P]], channel_multiplier=-1)
                    if i < TT - 1:
                        ch.inc(ins)
                return ins

            def mask_softplus(h):
                pool.wait_ge(s_sbsp, h + 1)
                mask(sb_sp[h % 2]).then_inc(s_sbspm, 1)

            mask_softplus(0)
            mask_softplus(1)
            for h in range(SB_HEADS):
                pool.wait_ge(s_sba, h + 1)
                mask(sb_w[h % 2]).then_inc(s_sbam, 1)
                if h + 2 < SB_HEADS:
                    mask_softplus(h + 2)

            wait_filled(pool, ("y2", 0, 0))
            imp = dict(allow_small_or_imprecise_dtypes=True)
            ch.inc(g.iota(iota_e, pattern=[[1, E]], base=0, channel_multiplier=0, **imp))
            ch.inc(g.iota(iota_o, pattern=[[1, 32]], base=0, channel_multiplier=0, **imp))
            ch.inc(g.iota(iota_c, pattern=[[1, C]], base=0, channel_multiplier=0, **imp))
            ch.inc(g.iota(tok_less, pattern=[[P, TT]], base=-T, channel_multiplier=1, **imp))
            ch.inc(g.iota(pad_row, pattern=[[0, 1]], base=T, channel_multiplier=1, **imp))
            ch.link(g.memset(earlier_e, 1.0))
            ch.link(g.affine_select(out=earlier_e, in_=earlier_e, compare_op=ALU.is_gt, fill=0.0, base=0,
                                    pattern=[[1, E], [-1, E]], channel_multiplier=0))
            pool.sem_inc(s_const, 1)

            pool.wait_ge(s_items, 1)
            n = pool.value_load(n_items_i[0:1, 0:1], min_val=E, max_val=MAX_ITEMS)

            def gather(t):
                if isinstance(t, int) and t == 0:
                    ch.link(g.tensor_copy(gather_idx, src_row[:, 0:1]))
                else:
                    pool.wait_ge(s_xt, t)
                    g.tensor_copy(gather_idx, src_row[:, bass.ds(t, 1)]).then_inc(s_gidx, 1)
                pool.wait_ge(s_rowsout, 16 * TT)
                if not (isinstance(t, int) and t == 0):
                    pool.wait_ge(s_gidx, t)
                g.indirect_dma_start(out=x_rows, out_offset=None, in_=rows_dram[:, :],
                                     in_offset=bass.IndirectOffsetOnAxis(gather_idx, 0))\
                    .then_inc(s_xrow, 16)

            def scatter(t):
                if not (isinstance(t, int) and t == 0):
                    pool.wait_ge(s_scat, 16 * t)
                g.tensor_copy(scatter_idx, acc_row[:, bass.ds(t, 1)]).then_inc(s_sidx, 1)
                pool.wait_ge(s_accinit, 16 * TT)
                pool.wait_ge(s_sidx, t + 1)
                pool.wait_ge(s_yrow, t + 1)
                g.indirect_dma_start(out=acc_dram[:, :],
                                     out_offset=bass.IndirectOffsetOnAxis(scatter_idx, 0),
                                     in_=y_rows, in_offset=None, compute_op=ALU.add).then_inc(s_scat, 16)

            gather(0)
            gather(1)
            scatter(0)
            with pool.Fori(1, n) as t:
                gather(t + 1)
                scatter(t)
            pool.wait_ge(s_scat, 16 * n)


_INS = ["x", "mem", "g_mix", "w_in", "w_gla_gate", "b_gla_gate", "g_gla_head", "w_out", "g_mem_q",
        "g_mem_kv", "w_mq", "w_mk", "w_mv", "w_mo", "g_ffn", "w_router", "b_router", "w_gu", "b_gu",
        "w_down", "b_down", "g_final"]


def kernel(**inputs):
    import concourse.bacc as bacc
    from concourse.bass_utils import run_bass_kernel_spmd

    nc = bacc.Bacc("TRN2", target_bir_lowering=False, num_devices=1)
    arrays, args = {}, []
    for name in _INS:
        a = np.ascontiguousarray(inputs[name])
        arrays[f"in_{name}"] = a
        args.append(nc.dram_tensor(f"in_{name}", a.shape, mybir.dt.from_np(a.dtype), kind="ExternalInput").ap())
    args.append(nc.dram_tensor("out", (1, T, D), F32, kind="ExternalOutput").ap())
    build(nc, *args)
    r = run_bass_kernel_spmd(nc, [arrays], core_ids=[0])
    return r.results[0]["out"]
```
